# Optimizing a Trainium2 kernel written in Bass

```python
import jax, jax.numpy as jnp
from jax import lax
import numpy as np

"""One inference step (DEPTH layers) of a hybrid autoregressive decoder, shared weights for two request groups.

Per layer: RMSNorm -> ONE combined input projection whose columns are split among
  (A) sliding-window grouped-query attention (window 128, rotary, learned per-head sinks, banded blocks) and
  (B) gated linear attention (GLA: low-rank data-dependent per-key-channel decay, chunked exact recurrence,
      per-head RMSNorm and swish output gate),
plus two per-channel sigmoid merge gates; each branch is projected to D_MODEL, merged by its gate, then one output
projection; residual add; RMSNorm -> hierarchical MoE (softmax over expert groups, top-1 group, then top-2 gated-MLP
experts within that group); residual add. One final RMSNorm.

Inputs:
  x_prompt (BATCH, SEQ, D_MODEL), positions 0..SEQ-1, fresh sequences
  x_sample (DEC_BATCH, DEC_SEQ, D_MODEL), positions PAST_LEN..PAST_LEN+DEC_SEQ-1
  cache_win_k, cache_win_v (DEPTH, DEC_BATCH, WINDOW, ATTN_KV_HEADS, HEAD_DIM): rotated keys / values of
      positions PAST_LEN-WINDOW..PAST_LEN-1
  state_gla (DEPTH, DEC_BATCH, GLA_HEADS, GLA_DK, GLA_DV): GLA recurrent matrix state after PAST_LEN tokens
Returns the tuple
  (y_prompt (BATCH, SEQ, D_MODEL), y_sample (DEC_BATCH, DEC_SEQ, D_MODEL),
   prompt_win_k, prompt_win_v (DEPTH, BATCH, WINDOW, ATTN_KV_HEADS, HEAD_DIM),
   prompt_gla_state (DEPTH, BATCH, GLA_HEADS, GLA_DK, GLA_DV),
   sample_win_k, sample_win_v (DEPTH, DEC_BATCH, WINDOW, ATTN_KV_HEADS, HEAD_DIM),
   sample_gla_state (DEPTH, DEC_BATCH, GLA_HEADS, GLA_DK, GLA_DV))
"""

D_MODEL = 1024
BATCH = 1
SEQ = 512
DEPTH = 1
DEC_BATCH = 8
DEC_SEQ = 4
PAST_LEN = 2048
PAGE_SIZE = 128

ATTN_HEADS = 8
ATTN_KV_HEADS = 2
GROUP = ATTN_HEADS // ATTN_KV_HEADS
HEAD_DIM = 64
ATTN_WIDTH = ATTN_HEADS * HEAD_DIM
KV_WIDTH = ATTN_KV_HEADS * HEAD_DIM
WINDOW = 128
ROPE_THETA = 10000.0
GLA_HEADS = 4
GLA_KEY_WIDTH = D_MODEL // 2
GLA_VALUE_WIDTH = D_MODEL
GLA_DK = GLA_KEY_WIDTH // GLA_HEADS
GLA_DV = GLA_VALUE_WIDTH // GLA_HEADS
GLA_GATE_RANK = 16
GLA_GATE_NORMALIZER = 16.0
GLA_CHUNK = 16
N_GROUPS = 4
EXPERTS_PER_GROUP = 8
N_EXPERTS = N_GROUPS * EXPERTS_PER_GROUP
TOP_K_IN_GROUP = 2
EXPERT_FF = 256
EPS = 1e-6
IN_PROJ_WIDTH = ATTN_WIDTH + 2 * KV_WIDTH + 2 * GLA_KEY_WIDTH + 2 * GLA_VALUE_WIDTH + GLA_GATE_RANK + 2 * D_MODEL

kernel_name = 'hybrid_swa_gla_hmoe_step'

def _rmsnorm(x, g):
    xf = x.astype(jnp.float32)
    y = xf * lax.rsqrt(jnp.mean(xf * xf, axis=-1, keepdims=True) + EPS)
    return (y * g.astype(jnp.float32)).astype(x.dtype)

def _split_points():
    widths = (ATTN_WIDTH, KV_WIDTH, KV_WIDTH, GLA_KEY_WIDTH, GLA_KEY_WIDTH,
              GLA_VALUE_WIDTH, GLA_VALUE_WIDTH, GLA_GATE_RANK, D_MODEL, D_MODEL)
    points, acc = [], 0
    for w in widths[:-1]:
        acc += w
        points.append(acc)
    return points

def _rope(x, positions):
    half = HEAD_DIM // 2
    inv_freq = ROPE_THETA ** (-jnp.arange(half, dtype=jnp.float32) / half)
    ang = positions.astype(jnp.float32)[:, None] * inv_freq[None, :]
    cos = jnp.cos(ang)[:, None, :]
    sin = jnp.sin(ang)[:, None, :]
    xf = x.astype(jnp.float32)
    x1, x2 = xf[..., :half], xf[..., half:]
    return jnp.concatenate([x1 * cos - x2 * sin, x2 * cos + x1 * sin], axis=-1).astype(x.dtype)

def _sink_softmax(s, mask, sinks):
    s = jnp.where(mask, s, -jnp.inf)
    sink = jnp.broadcast_to(sinks.astype(jnp.float32).reshape(ATTN_KV_HEADS, GROUP, 1, 1), s.shape[:-1] + (1,))
    p = jax.nn.softmax(jnp.concatenate([s, sink], axis=-1), axis=-1)
    return p[..., :-1]

def _swa_prompt(q, k, v, sinks):
    B, T = q.shape[0], q.shape[1]
    nb = T // WINDOW
    qb = q.reshape(B, nb, WINDOW, ATTN_KV_HEADS, GROUP, HEAD_DIM)

    def with_prev(xb):
        xb = xb.reshape(B, nb, WINDOW, ATTN_KV_HEADS, HEAD_DIM)
        prev = jnp.pad(xb[:, :-1], ((0, 0), (1, 0), (0, 0), (0, 0), (0, 0)))
        return jnp.concatenate([prev, xb], axis=2)

    kk, vv = with_prev(k), with_prev(v)
    s = jnp.einsum('bnqkgd,bnskd->bnkgqs', qb, kk, preferred_element_type=jnp.float32) * (HEAD_DIM ** -0.5)
    q_pos = jnp.arange(WINDOW)[:, None]
    k_pos = jnp.arange(2 * WINDOW)[None, :] - WINDOW
    rel = q_pos - k_pos
    blk = jnp.arange(nb)[:, None, None]
    mask = (rel >= 0) & (rel <= WINDOW) & (blk * WINDOW + k_pos >= 0)
    p = _sink_softmax(s, mask[:, None, None], sinks)
    o = jnp.einsum('bnkgqs,bnskd->bnqkgd', p.astype(v.dtype), vv)
    return o.reshape(B, T, ATTN_WIDTH)

def _swa_sample(q, k, v, cache_k, cache_v, sinks):
    B, T = q.shape[0], q.shape[1]
    kk = jnp.concatenate([cache_k.astype(k.dtype), k], axis=1)
    vv = jnp.concatenate([cache_v.astype(v.dtype), v], axis=1)
    qg = q.reshape(B, T, ATTN_KV_HEADS, GROUP, HEAD_DIM)
    s = jnp.einsum('bqkgd,bskd->bkgqs', qg, kk, preferred_element_type=jnp.float32) * (HEAD_DIM ** -0.5)
    rel = (jnp.arange(T)[:, None] + WINDOW) - jnp.arange(WINDOW + T)[None, :]
    mask = (rel >= 0) & (rel <= WINDOW)
    p = _sink_softmax(s, mask, sinks)
    o = jnp.einsum('bkgqs,bskd->bqkgd', p.astype(v.dtype), vv).reshape(B, T, ATTN_WIDTH)
    return o, kk[:, -WINDOW:], vv[:, -WINDOW:]

def _gla_scan(q, k, v, log_a, s0):
    B, T, H, _ = q.shape
    DV = v.shape[-1]
    pad = (-T) % GLA_CHUNK
    nc = (T + pad) // GLA_CHUNK

    def chunks(a):
        a = jnp.pad(a.astype(jnp.float32), ((0, 0), (0, pad), (0, 0), (0, 0)))
        return a.reshape(B, nc, GLA_CHUNK, H, a.shape[-1]).transpose(1, 0, 3, 2, 4)

    causal = jnp.tril(jnp.ones((GLA_CHUNK, GLA_CHUNK), dtype=bool))[:, :, None]

    def step(S, inp):
        qc, kc, vc, ac = inp
        b = jnp.cumsum(ac, axis=2)
        b_last = b[:, :, -1:]
        decay = jnp.exp(jnp.where(causal, b[:, :, :, None] - b[:, :, None], -jnp.inf))
        A = jnp.einsum('bhtd,bhsd,bhtsd->bhts', qc, kc, decay)
        o = jnp.einsum('bhts,bhsv->bhtv', A, vc) + jnp.einsum('bhtd,bhdv->bhtv', qc * jnp.exp(b), S)
        S = jnp.exp(b_last[:, :, 0, :, None]) * S + jnp.einsum('bhsd,bhsv->bhdv', kc * jnp.exp(b_last - b), vc)
        return S, o

    S, o = lax.scan(step, s0.astype(jnp.float32), (chunks(q), chunks(k), chunks(v), chunks(log_a)))
    o = o.transpose(1, 0, 3, 2, 4).reshape(B, nc * GLA_CHUNK, H, DV)[:, :T]
    return o, S

def _gla(q, k, v, f_lr, r, s0, w_f2, b_f, norm_g):
    B, T = q.shape[0], q.shape[1]
    log_a = jax.nn.log_sigmoid((f_lr @ w_f2 + b_f).astype(jnp.float32)) / GLA_GATE_NORMALIZER
    qh = q.reshape(B, T, GLA_HEADS, GLA_DK) * (GLA_DK ** -0.5)
    kh = k.reshape(B, T, GLA_HEADS, GLA_DK)
    vh = v.reshape(B, T, GLA_HEADS, GLA_DV)
    o, S = _gla_scan(qh, kh, vh, log_a.reshape(B, T, GLA_HEADS, GLA_DK), s0)
    o = _rmsnorm(o, norm_g) * jax.nn.silu(r.reshape(B, T, GLA_HEADS, GLA_DV).astype(jnp.float32))
    return o.reshape(B, T, GLA_VALUE_WIDTH).astype(q.dtype), S

def _moe(h, w_rg, b_rg, w_re, b_re, w_eg, w_eu, w_ed):
    lead = h.shape[:-1]
    hf = h.reshape(-1, D_MODEL)
    n = hf.shape[0]
    p_group = jax.nn.softmax((hf @ w_rg + b_rg).astype(jnp.float32), axis=-1)
    g_star = jnp.argmax(p_group, axis=-1)
    p_sel = jnp.take_along_axis(p_group, g_star[:, None], axis=-1)
    e_logits = (hf @ w_re + b_re).astype(jnp.float32).reshape(n, N_GROUPS, EXPERTS_PER_GROUP)
    e_sel = jnp.take_along_axis(e_logits, g_star[:, None, None], axis=1)[:, 0]
    top_v, top_i = lax.top_k(e_sel, TOP_K_IN_GROUP)
    w_top = jax.nn.softmax(top_v, axis=-1) * p_sel
    expert = g_star[:, None] * EXPERTS_PER_GROUP + top_i
    combine = jnp.sum(jax.nn.one_hot(expert, N_EXPERTS, dtype=jnp.float32) * w_top[..., None], axis=1)
    combine = combine.astype(hf.dtype)
    out = jnp.zeros_like(hf)
    for g in range(N_GROUPS):
        sl = slice(g * EXPERTS_PER_GROUP, (g + 1) * EXPERTS_PER_GROUP)
        a = jnp.einsum('nd,edf->nef', hf, w_eg[sl])
        u = jnp.einsum('nd,edf->nef', hf, w_eu[sl])
        act = jax.nn.silu(a) * u * combine[:, sl, None]
        out = out + jnp.einsum('nef,efd->nd', act, w_ed[sl])
    return out.reshape(lead + (D_MODEL,))

def _layer(x, positions, cache_k, cache_v, gla_state, norm_mix, w_in, w_gla_f2, b_gla_f, gla_norm,
           attn_sinks, w_proj_attn, w_proj_gla, w_out, norm_ffn, w_router_group, b_router_group,
           w_router_expert, b_router_expert, w_exp_gate, w_exp_up, w_exp_down):
    B, T = x.shape[0], x.shape[1]
    h = _rmsnorm(x, norm_mix)
    q_a, k_a, v_a, q_g, k_g, v_g, r_g, f_lr, gate_a, gate_b = jnp.split(h @ w_in, _split_points(), axis=-1)
    q_a = _rope(q_a.reshape(B, T, ATTN_HEADS, HEAD_DIM), positions)
    k_a = _rope(k_a.reshape(B, T, ATTN_KV_HEADS, HEAD_DIM), positions)
    v_a = v_a.reshape(B, T, ATTN_KV_HEADS, HEAD_DIM)
    if cache_k is None:
        a_out = _swa_prompt(q_a, k_a, v_a, attn_sinks)
        new_k, new_v = k_a[:, -WINDOW:], v_a[:, -WINDOW:]
        s0 = jnp.zeros((B, GLA_HEADS, GLA_DK, GLA_DV), jnp.float32)
    else:
        a_out, new_k, new_v = _swa_sample(q_a, k_a, v_a, cache_k, cache_v, attn_sinks)
        s0 = gla_state
    g_out, new_s = _gla(q_g, k_g, v_g, f_lr, r_g, s0, w_gla_f2, b_gla_f, gla_norm)
    merged = jax.nn.sigmoid(gate_a) * (a_out @ w_proj_attn) + jax.nn.sigmoid(gate_b) * (g_out @ w_proj_gla)
    x = x + merged @ w_out
    x = x + _moe(_rmsnorm(x, norm_ffn), w_router_group, b_router_group, w_router_expert, b_router_expert,
                 w_exp_gate, w_exp_up, w_exp_down)
    return x, new_k, new_v, new_s

def setup_inputs(seed: int = 0) -> dict:
    key = jax.random.key(seed)
    ks = jax.random.split(key, 24)
    f32 = jnp.float32
    L = DEPTH

    def nrm(k, shape, scale):
        return jax.random.normal(k, shape, f32) * scale

    return {
        'x_prompt': nrm(ks[0], (BATCH, SEQ, D_MODEL), 1.0),
        'x_sample': nrm(ks[1], (DEC_BATCH, DEC_SEQ, D_MODEL), 1.0),
        'cache_win_k': nrm(ks[2], (L, DEC_BATCH, WINDOW, ATTN_KV_HEADS, HEAD_DIM), 1.0),
        'cache_win_v': nrm(ks[3], (L, DEC_BATCH, WINDOW, ATTN_KV_HEADS, HEAD_DIM), 1.0),
        'state_gla': nrm(ks[4], (L, DEC_BATCH, GLA_HEADS, GLA_DK, GLA_DV), 0.5),
        'norm_mix': 1.0 + nrm(ks[5], (L, D_MODEL), 0.02),
        'w_in': nrm(ks[6], (L, D_MODEL, IN_PROJ_WIDTH), D_MODEL ** -0.5),
        'w_gla_f2': nrm(ks[7], (L, GLA_GATE_RANK, GLA_KEY_WIDTH), GLA_GATE_RANK ** -0.5),
        'b_gla_f': nrm(ks[8], (L, GLA_KEY_WIDTH), 0.1),
        'gla_norm': 1.0 + nrm(ks[9], (L, GLA_DV), 0.02),
        'attn_sinks': nrm(ks[10], (L, ATTN_HEADS), 0.5),
        'w_proj_attn': nrm(ks[11], (L, ATTN_WIDTH, D_MODEL), ATTN_WIDTH ** -0.5),
        'w_proj_gla': nrm(ks[12], (L, GLA_VALUE_WIDTH, D_MODEL), GLA_VALUE_WIDTH ** -0.5),
        'w_out': nrm(ks[13], (L, D_MODEL, D_MODEL), D_MODEL ** -0.5),
        'norm_ffn': 1.0 + nrm(ks[14], (L, D_MODEL), 0.02),
        'w_router_group': nrm(ks[15], (L, D_MODEL, N_GROUPS), D_MODEL ** -0.5),
        'b_router_group': nrm(ks[16], (L, N_GROUPS), 0.01),
        'w_router_expert': nrm(ks[17], (L, D_MODEL, N_EXPERTS), D_MODEL ** -0.5),
        'b_router_expert': nrm(ks[18], (L, N_EXPERTS), 0.01),
        'w_exp_gate': nrm(ks[19], (L, N_EXPERTS, D_MODEL, EXPERT_FF), D_MODEL ** -0.5),
        'w_exp_up': nrm(ks[20], (L, N_EXPERTS, D_MODEL, EXPERT_FF), D_MODEL ** -0.5),
        'w_exp_down': nrm(ks[21], (L, N_EXPERTS, EXPERT_FF, D_MODEL), EXPERT_FF ** -0.5),
        'norm_final': 1.0 + nrm(ks[22], (D_MODEL,), 0.02),
    }

def reference(x_prompt, x_sample, cache_win_k, cache_win_v, state_gla, norm_mix, w_in, w_gla_f2, b_gla_f,
              gla_norm, attn_sinks, w_proj_attn, w_proj_gla, w_out, norm_ffn, w_router_group, b_router_group,
              w_router_expert, b_router_expert, w_exp_gate, w_exp_up, w_exp_down, norm_final):
    pos_prompt = jnp.arange(x_prompt.shape[1], dtype=jnp.int32)
    pos_sample = PAST_LEN + jnp.arange(x_sample.shape[1], dtype=jnp.int32)
    yp, ys = x_prompt, x_sample
    pk, pv, ps, sk, sv, ss = [], [], [], [], [], []
    for l in range(DEPTH):
        lw = (norm_mix[l], w_in[l], w_gla_f2[l], b_gla_f[l], gla_norm[l], attn_sinks[l], w_proj_attn[l],
              w_proj_gla[l], w_out[l], norm_ffn[l], w_router_group[l], b_router_group[l], w_router_expert[l],
              b_router_expert[l], w_exp_gate[l], w_exp_up[l], w_exp_down[l])
        yp, k1, v1, s1 = _layer(yp, pos_prompt, None, None, None, *lw)
        ys, k2, v2, s2 = _layer(ys, pos_sample, cache_win_k[l], cache_win_v[l], state_gla[l], *lw)
        pk.append(k1)
        pv.append(v1)
        ps.append(s1)
        sk.append(k2)
        sv.append(v2)
        ss.append(s2)
    y_prompt = _rmsnorm(yp, norm_final)
    y_sample = _rmsnorm(ys, norm_final)
    prompt_win_k = jnp.stack(pk)
    prompt_win_v = jnp.stack(pv)
    prompt_gla_state = jnp.stack(ps)
    sample_win_k = jnp.stack(sk)
    sample_win_v = jnp.stack(sv)
    sample_gla_state = jnp.stack(ss)
    return (y_prompt, y_sample, prompt_win_k, prompt_win_v, prompt_gla_state, sample_win_k, sample_win_v, sample_gla_state)


_drawn_inputs = setup_inputs


def setup_inputs(seed=0):
    import zlib

    import numpy as np

    out = dict(_drawn_inputs(seed))
    spreads = {}
    factors = {'gla_norm': 3.848,
     'attn_sinks': 8.0,
     'b_router_group': 14.817,
     'b_router_expert': 3.118,
     'norm_final': 7.961}
    for name, (base, spread) in spreads.items():
        noise = np.random.default_rng([zlib.crc32(name.encode()), seed]).standard_normal(out[name].shape)
        drawn = base * np.exp(spread * noise) if base else spread * noise
        out[name] = __import__('jax').numpy.asarray(drawn.astype(out[name].dtype))
    for name, factor in factors.items():
        out[name] = (out[name] * factor).astype(out[name].dtype)
    return out
```

```python
import concourse.bass as bass
from concourse import mybir
from contextlib import ExitStack
import numpy as np

D, NTOK, NPROMPT, NB = 1024, 544, 512, 5
KC = D // 128
AH, KVH, HD, M4 = 8, 2, 64, 4
GH, DK, DV = 4, 128, 256
DB, DS, WIN = 8, 4, 128
NE, NG, EPG, FF = 32, 4, 8, 256
EPS = 1e-6
HALF = NTOK // 2
PADTOK = 640
CAP = 64
NFIX = NE // 2
MAXOV = (2 * NTOK) // CAP + 3
OVH = MAXOV // 2
NPC = NFIX + OVH + 1
NOTOK = 4096
COLS = dict(q=0, k=512, v=640, qg=768, kg=1280, vg=1792, rg=2816, f=3840, ga=3856, gb=4880)


def shape_constants():
    p = np.arange(128)
    f = np.float32
    parts = {}
    parts["ident"] = np.eye(128)
    parts["causal"] = (p[None, :] <= p[:, None])
    parts["ones"] = np.ones((128, 128))
    parts["before"] = (p[:, None] < p[None, :])
    kk = np.arange(256)[None, :]
    parts["window"] = np.where((kk >= p[:, None]) & (kk <= p[:, None] + WIN), 0.0, -1e30)
    t = np.arange(NTOK)
    start = np.where(t < NPROMPT, t % 128 == 0, (t - NPROMPT) % DS == 0)
    parts["scan"] = np.broadcast_to(1.0 - start, (128, NTOK))
    s = np.arange(32)
    parts["of_batch"] = np.broadcast_to((s[None, :] // DS == np.arange(DB)[:, None]).reshape(1, -1), (128, 256))
    parts["row_batch"] = (p[:, None] // DS == np.arange(DB)[None, :])
    parts["s_causal"] = (s[None, :] // DS == p[:, None] // DS) & (s[None, :] <= p[:, None])
    tq = (p % DS)[:, None]
    parts["s_old"] = np.where(np.arange(WIN)[None, :] >= tq, 0.0, -1e30)
    new_ok = (s[None, None, :] // DS == np.arange(DB)[None, :, None]) & ((s % DS)[None, None, :] <= tq[:, :, None])
    parts["s_new"] = np.where(new_ok, 0.0, -1e30).reshape(128, 256)
    parts["rev4"] = np.broadcast_to(NG - np.arange(NG), (128, NG))
    parts["rev32"] = np.broadcast_to(NE - np.arange(NE), (128, NE))
    e = np.arange(NE)
    parts["place"] = np.broadcast_to((e % 2) * CAP * NPC + e // 2, (128, NE))
    parts["expert"] = np.broadcast_to(e, (128, NE))
    parts["steps"] = np.broadcast_to(CAP * np.arange(1, 9), (128, 8))
    parts["ovtile"] = np.broadcast_to(np.arange(MAXOV), (128, MAXOV))
    parts["pairsteps"] = np.broadcast_to(2 * np.arange(OVH // 2), (128, OVH // 2))
    parts["valid"] = (np.arange(NB)[None, :] * 128 + p[:, None] < NTOK)
    at, where, cols = 0, {}, []
    for n, a in parts.items():
        where[n] = (at, a.shape[1])
        at += a.shape[1]
        cols.append(a.astype(f))
    tables = np.concatenate(cols, 1)
    pos = np.concatenate([np.arange(NPROMPT), 2048 + np.arange(32) % DS, np.zeros(96)]).astype(f)
    inv = (f(10000.0) ** (-np.arange(32, dtype=f) / f(32))).astype(f)
    ang = (pos[:, None] * inv[None, :]).astype(f).astype(np.float64)
    c, sn = np.cos(ang).astype(f), np.sin(ang).astype(f)
    rope = np.stack([np.concatenate([c, c], 1), np.concatenate([-sn, sn], 1)])
    rope = rope.reshape(2, NB, 128, 64).transpose(2, 0, 1, 3).reshape(128, -1)
    ids = np.minimum(np.arange(NB)[None, :] * 128 + p[:, None], NTOK - 1)
    rows = np.concatenate([ids, ids + NTOK], 1).astype(np.int32)
    empty = np.full((CAP * 2 * NPC, 1), NOTOK, np.int32)
    return where, tables, np.ascontiguousarray(rope), rows, empty


KOFF = (0, 32, 96, 192)


def decoder_step(nc, a, o):
    F, R, I = mybir.dt.float32, mybir.dt.float32r, mybir.dt.int32
    ALU, ACT, AX = mybir.AluOpType, mybir.ActivationFunctionType, mybir.AxisListType
    where, tables, _, _, _ = shape_constants()
    NCONST = tables.shape[1]
    BASE = 16640
    H0 = BASE
    D0 = H0 + 40960
    W0 = D0 + 106240
    C0 = W0 + 49152
    used = [C0]

    def at(name, shape, dt, offset):
        return nc.alloc_sbuf_tensor_at(name, shape, dt, offset=offset)

    def small(name, shape, dt=F):
        n = int(np.prod(shape[1:])) * 4
        off = used[0]
        used[0] += (n + 31) // 32 * 32
        return at(name, shape, dt, off)

    HT = at("hT_split", [128, 2, KC, PADTOK], R, H0)
    AT = at("attn_outT_split", [128, 2, M4, NTOK], R, D0)
    QKG = at("gla_qkT", [128, 8, NTOK], F, D0 + 17408)
    LA = at("gla_log_decay", [128, GH, NTOK], F, D0 + 34816)
    GT = at("gla_outT_split", [128, 2, KC, NTOK], R, D0 + 17408)
    SG = at("merge_gates", [128, 2, 2, NTOK], F, D0 + 52224)
    MTMP = at("merge_tmp", [128, 2, NTOK], F, D0 + 60928)
    MT = at("mergedT_split", [128, 2, KC, PADTOK], R, D0 + 65280)
    VG = at("gla_v", [128, NB, 1024], F, D0 + 85760)
    XS = at("x_rows", [128, NB, D], F, D0 + 85760)
    HS = at("h_rows", [128, 2, D], F, D0 + 43520)
    NMIX = at("norm_mix_rows", [128, D], F, D0 + 51712)
    JUNK = at("square_junk", [128, D], F, D0 + 55808)
    QK = at("qk_rotated", [128, NB, 640], F, D0 + 43520)
    SC = at("scores", [128, 2, 4, 256], F, D0 + 43520)
    PT = at("probsT", [128, 2, 512], F, D0 + 51712)
    VT = at("attn_v", [128, NB, 128], F, D0 + 56320)
    QT = at("attn_qT", [128, M4, NTOK], F, D0 + 58880)
    KT = at("attn_kT", [128, NTOK], F, D0 + 67584)
    VC = at("cache_v_rows", [128, DB, 128], F, D0 + 69760)
    RT = at("rope_tmp", [128, 2, 512], F, D0 + 73856)
    ROPE = at("rope_tables", [128, 2, NB, 64], F, D0 + 77952)
    FLT = at("gate_lowrankT", [16, NTOK], F, D0 + 73856)
    ZT = at("decay_tmp", [128, GH, NTOK], F, D0 + 77056)
    SS = at("s_scores", [16, 16, 160], F, D0 + 85760)
    CK = at("cache_k_rows", [128, DB, 128], F, D0 + 96000)
    CKT = at("cache_kT", [128, DB, 128], F, D0 + 100096)
    PTO = at("s_probsT_old", [128, 256], F, D0 + 104192)
    PTN = at("s_probsT_new", [32, 256], F, D0 + 105216)
    ST = at("gla_state", [128, GH, DV], F, D0 + 43520)
    KD = at("k_decays", [128, 1280], F, D0 + 47616)
    KTL = at("k_tilde", [128, 1280], F, D0 + 52736)
    QD = at("q_decays", [128, GH, 128], F, D0 + 57856)
    QTL = at("q_tilde", [128, GH, 128], F, D0 + 59904)
    QB = at("q_from_start", [128, GH, 128], F, D0 + 61952)
    KH = at("k_to_end", [128, GH, 128], F, D0 + 64000)
    KHR = at("k_to_end_rows", [128, GH, 128], F, D0 + 66048)
    AM = at("gla_attn", [128, GH, 128], F, D0 + 68096)
    AMT = at("gla_attnT", [128, GH, 128], F, D0 + 70144)
    RO = at("r_silu", [128, 3, 512], F, D0 + 72192)
    RL = at("r_silu_rows", [128, D], F, D0 + 72192)
    RLS = at("s_r_silu_rows", [32, D], F, D0 + 43520)
    OJ = at("o_square_junk", [128, DV], F, D0 + 82432)
    S0 = at("s_state_a", [128, DB, DV], F, D0 + 47616)
    S1 = at("s_state_b", [128, DB, DV], F, D0 + 57856)
    SMQ = at("s_q_masked", [128, GH, DB, 32], F, D0 + 43520)
    SKM = at("s_k_masked", [32, DB, 128], F, D0 + 78336)
    SQB = at("s_q_from_start", [128, GH, 32], F, D0 + 83456)
    SKT = at("s_k_tilde", [128, GH, 32], F, D0 + 83968)
    SKH = at("s_k_to_end", [128, GH, 32], F, D0 + 84480)
    SEX = at("s_exp", [128, GH, 32], F, D0 + 84992)
    RAW = at("w_raw", [128, 2, 2048], F, W0)
    WS = at("w_split", [128, 2, 2, 2048], R, W0 + 16384)
    X2 = at("x_after_mix", [128, NB, D], F, H0)
    WGU = [at(f"expert_gate_up_{u}", [128, 2, KC, 2, FF], F, H0 + 20480 + 49152 * u) for u in range(2)]
    WDN = [at(f"expert_down_{u}", [128, 2, 2, D], F, H0 + 20480 + 49152 * u + 32768) for u in range(2)]
    T0 = H0 + 20480 + 98304
    NFFN = at("norm_ffn_rows", [128, D], F, T0)
    H2 = at("h2_rows", [128, 2, D], F, T0 + 4096)
    H2T = at("h2T", [128, KC, NTOK], F, T0 + 12288)
    LT = at("logitsT", [36, NTOK], F, T0 + 33792)
    XG = [at(f"gathered_{u}", [128, D], F, T0 + 36864 + 4096 * u) for u in range(2)]
    XT = [at(f"gatheredT_{u}", [128, KC, 128], F, T0 + 45056 + 4096 * u) for u in range(2)]
    YO = [at(f"expert_out_{u}", [128, D], F, T0 + 53248 + 4096 * u) for u in range(2)]
    AC = [at(f"expert_act_{u}", [128, FF], F, T0 + 61440 + 1024 * u) for u in range(2)]
    SA = at("expert_silu", [128, FF], F, T0 + 63488)
    ACTT = [at(f"expert_actT_{u}", [128, 2, 128], F, T0 + 64512 + 1024 * u) for u in range(2)]
    RR = [at(f"route_{n}", [128, NB, NE], F, T0 + 66560 + 640 * n) for n in range(12)]
    CMP = at("route_compare", [128, MAXOV * NE], F, T0)
    YI = [at(f"token_out_{n}", [128, D], F, H0 + 20480 + 4096 * n) for n in range(2 * NB)]
    NFIN = at("norm_final_rows", [128, D], F, T0 + 24576)
    JUNK3 = at("square_junk3", [128, D], F, T0 + 28672)

    CF = small("tables", [128, NCONST])

    def cst(name):
        s, n = where[name]
        return CF[:, s:s + n]

    GN = small("gla_norm_rows", [128, DV])
    BG = small("decay_bias", [128, GH])
    SINK = small("sinks_rows", [128, AH])
    SINKS = small("sinks_sample", [16, KVH])
    WR = small("router_w", [128, KC, 36])
    RB = small("router_bias", [128, 36])
    WF2 = small("decay_w2", [16, 512])
    SSQ = small("sum_squares", [128, NB])
    SSH = small("sum_squares_halves", [128, 2, NB])
    RST = small("rstd", [128, NB])
    OSQ = small("o_sum_squares", [128, NB, GH])
    ORS = small("o_rstd", [128, NB, GH])
    MX = small("row_max", [128, 2, 4])
    NMX = small("neg_row_max", [128, 2, 4])
    SUM = small("row_sum", [128, 2, 4])
    ESK = small("sink_exp", [128, 2, 4])
    DEN = small("denominators", [128, 2, 4])
    SQT = small("s_qT", [128, DB, 16])
    SMX = small("s_row_max", [16, 16])
    SSK = small("s_sink_exp", [16, 16])
    SSM = small("s_row_sum", [16, 16])
    EBL = small("chunk_decay", [128, GH])
    SEBL = small("s_chunk_decay", [128, GH, DB])
    ROWID = small("token_rows", [128, 2 * NB], I)
    late_used = [T0 + 74240]

    def late(name, shape, dt=F):
        off = late_used[0]
        late_used[0] += (int(np.prod(shape[1:])) * 4 + 31) // 32 * 32
        return at(name, shape, dt, off)

    RG = [late(f"route_g{n}", [128, NB, NG]) for n in range(4)]
    R1 = {n: late("route_" + n, [128, NB]) for n in
          ("gmax", "grev", "gsum", "psel", "v1", "m1", "v2", "m2", "d", "e2", "w1", "w2")}
    R2 = {n: late("slot_" + n, [128, 2 * NB]) for n in ("rank", "place", "over", "q", "row", "isov", "tile", "half", "pos", "a")}
    RE1 = {n: late("expert_" + n, [128, NE]) for n in ("count", "tiles", "cum", "start")}
    POSI = late("slot_pos", [128, 2 * NB], I)
    IDXS = late("scatter_rows", [128, NPC], I)
    IDXG = late("gather_rows", [128, NPC], I)
    IF1 = late("rows_f", [128, NPC])
    IF2 = late("rows_f2", [128, NPC])
    ETF = late("pair_experts_f", [1, NPC, 2])
    ETI = late("pair_experts", [1, NPC, 2], I)
    EOV = late("overflow_experts", [1, MAXOV])
    ITF = late("iterations_f", [1, 1])
    ITI = late("iterations", [1, 1], I)
    ICG = [late(f"gather_column_{u}", [128, 1], I) for u in range(2)]
    ICS = [late(f"scatter_column_{u}", [128, 1], I) for u in range(2)]
    assert late_used[0] <= C0, late_used[0] - C0
    assert used[0] <= 229344, used[0]
    ident = cst("ident")

    rsilu_d = nc.dram_tensor("rsilu_scratch", [NB, 128, D], F, kind="Internal").ap()
    h2_d = nc.dram_tensor("h2_scratch", [NTOK, D], F, kind="Internal").ap()
    slot_d = nc.dram_tensor("slot_table", [2 * CAP * NPC, 1], I, kind="Internal").ap()
    tok_d = nc.dram_tensor("token_out_scratch", [2 * NTOK, D], F, kind="Internal").ap()

    win = a["w_in"][0]
    xp, xs = a["x_prompt"][0], a["x_sample"].rearrange("b t d -> (b t) d")

    def rows(bl):
        return 128 if bl < 4 else 32

    def xrows(bl):
        return xp[bl * 128:(bl + 1) * 128, :] if bl < 4 else xs

    def raw(u):
        return RAW[:, u % 2, :]

    def token_unit(u, c0, half):
        src = win if u < 32 else a["w_out"][0]
        return [(raw(u).rearrange("p (k n) -> p k n", n=512),
                 src[half * 512:(half + 1) * 512, c0:c0 + 512].rearrange("(k p) n -> p k n", p=128))]

    def unit_loads(u):
        if u < 2:
            return token_unit(u, 0, u)
        if u == 2:
            return [(raw(u).rearrange("p (k n) -> p k n", n=256), win[:, 512:768].rearrange("(k p) n -> p k n", p=128))]
        if u == 3:
            return [(raw(u)[:, 0:1024].rearrange("p (k n) -> p k n", n=128),
                     win[:, COLS["f"]:COLS["f"] + 128].rearrange("(k p) n -> p k n", p=128))]
        if u < 8:
            c = COLS["qg"] + 256 * (u - 4)
            return [(raw(u).rearrange("p (k n) -> p k n", n=256), win[:, c:c + 256].rearrange("(k p) n -> p k n", p=128))]
        if u < 12:
            return token_unit(u, COLS["vg"] + 512 * ((u - 8) // 2), (u - 8) % 2)
        if u < 16:
            return token_unit(u, COLS["rg"] + 512 * ((u - 12) // 2), (u - 12) % 2)
        if u < 32:
            j = (u - 16) // 2
            if u % 2 == 0:
                dst = raw(u).rearrange("p (k g n) -> p k g n", k=KC, g=2)
                return [(dst[:, :, g, :], win[:, c + 128 * j:c + 128 * j + 128].rearrange("(k p) n -> p k n", p=128))
                        for g, c in ((0, COLS["ga"]), (1, COLS["gb"]))]
            dst = raw(u)[:, 0:1536].rearrange("p (k n) -> p k n", n=128)
            pa, pg = a["w_proj_attn"][0], a["w_proj_gla"][0]
            out = [(dst[64 * g:64 * g + 64, 0:4, :],
                    pa[256 * g:256 * g + 256, 128 * j:128 * j + 128].rearrange("(m d) n -> d m n", d=64)) for g in range(2)]
            return out + [(dst[:, 4:12, :], pg[:, 128 * j:128 * j + 128].rearrange("(k p) n -> p k n", p=128))]
        return token_unit(u, 512 * ((u - 32) // 2), (u - 32) % 2)

    NU = 36

    def unit_size(u):
        return 1024 if u == 3 else 1536 if 16 <= u < 32 and u % 2 else 2048

    unit_full = []
    total = [0, 0]
    for u in range(NU):
        total[u % 2] += 16 * len(unit_loads(u))
        unit_full.append(total[u % 2])

    def main_steps(u):
        if u in (0, 1, 2) or 8 <= u < 16 or u >= 32:
            return NB
        return 1 if u == 3 or (u >= 16 and u % 2) else 2

    side = {}
    for bl in range(4):
        side[(2, bl + 1)] = [("T", bl)]
    side[(3, 0)] = [("T", 4), ("CT", 0), ("CT", 1), ("Z", 0)]
    bslots = [(u, s) for u in range(4, 8) for s in range(2)]
    cslots = [(u, s) for u in range(8, 12) for s in range(NB)]
    dslots = [(u, s) for u in range(12, 16) for s in range(NB)]
    for r in range(4):
        side[bslots[r]] = [("SQ", r)]
    side[bslots[4]] = [("ST", 0)]
    side[bslots[5]] = [("SV", 0)]
    side[bslots[6]] = [("QS", 0)]
    side[bslots[7]] = [("QS", 1)]
    for n in range(8):
        side[cslots[2 * n]] = [("QT", n)]
        side[cslots[2 * n + 1]] = [("QV", n)] + ([("QS", n + 2)] if n < 6 else [])
    side[cslots[19]] = [("GP", 0)]
    for n in range(4):
        for st in range(5):
            side[dslots[5 * n + st]] = [("G", n, st)]

    def side_steps(u, s):
        return side.get((u, s), [])

    kw = dict
    with ExitStack() as ctx:
        P = [ctx.enter_context(nc.psum_tensor(f"bank{i}", [128, 512], F)) for i in range(8)]

        def sem(name):
            return ctx.enter_context(nc.semaphore(name))

        tables_in, params_in, norm_in = sem("tables_in"), sem("params_in"), sem("norm_in")
        x_in = [sem(f"x_in{i}") for i in range(NB)]
        rope_in, cache_in = sem("rope_in"), sem("cache_in")
        raw_in = [sem("raw_in0"), sem("raw_in1")]
        hi_done, lo_done = sem("hi_done"), sem("lo_done")
        memset_done = sem("memset_done")
        squares, variance, root, h_rows = sem("squares"), sem("variance"), sem("root"), sem("h_rows")
        h_turned, h_hi, h_lo = sem("h_turned"), sem("h_hi"), sem("h_lo")
        main_mm = sem("main_mm")
        q_roped, k_roped, v_copied = sem("q_roped"), sem("k_roped"), sem("v_copied")
        low_out, z_mm, z_out, z_abs, z_ln, decay_ready = (sem(n) for n in ("low_out", "z_mm", "z_out", "z_abs", "z_ln", "decay_ready"))
        qg_out, vg_out, r_silu = (sem(n) for n in ("qg_out", "vg_out", "r_silu"))
        r_ready = sem("r_ready")
        r_spilled = [sem(f"r_spilled{i}") for i in range(3)]
        qk_turned, qk_out, ck_turned, ck_out = (sem(n) for n in ("qk_turned", "qk_out", "ck_turned", "ck_out"))
        dve_step = sem("dve_step")
        sq_mm, sq_out, s_exp, s_norm, s_exp_in = (sem(n) for n in ("sq_mm", "sq_out", "s_exp", "s_norm", "s_exp_in"))
        sp_turned, sp_out, sv_mm, at_hi, at_lo = (sem(n) for n in ("sp_turned", "sp_out", "sv_mm", "at_hi", "at_lo"))
        sc_out = sem("sc_out")
        qs_mm, qs_max, qs_exp, qs_norm, qs_turned, pt_out, qv_mm = (
            sem(n) for n in ("qs_mm", "qs_max", "qs_exp", "qs_norm", "qs_turned", "pt_out", "qv_mm"))
        kv_stored, win_stored = sem("kv_stored"), sem("win_stored")
        (k_arg, k_exp, kq_ready, b_arg, b_exp, b_ready) = (sem(n) for n in ("k_arg", "k_exp", "kq_ready", "b_arg", "b_exp", "b_ready"))
        (ga_mm, ga_out, gk_turned, gk_out, gat_turned, gat_out, gd_mm, go_out, gu_out) = (
            sem(n) for n in ("ga_mm", "ga_out", "gk_turned", "gk_out", "gat_turned", "gat_out", "gd_mm", "go_out", "gu_out"))
        pstate_stored = sem("pstate_stored")
        s_arg, s_exps, s_ready = sem("s_arg"), sem("s_exps"), sem("s_ready")
        sa_mm, sa_out, sk_turned, sk_out, sat_turned, sat_out = (
            sem(n) for n in ("sa_mm", "sa_out", "sk_turned", "sk_out", "sat_turned", "sat_out"))
        so_mm, so_out, skm_ready, su_mm, su_out = (sem(n) for n in ("so_mm", "so_out", "skm_ready", "su_mm", "su_out"))
        state_in = [sem("state_in0"), sem("state_in1")]
        state_stored = [sem("state_stored0"), sem("state_stored1")]
        o_squares = sem("o_squares")
        g_rows, g_turned, gt_hi, gt_lo = (sem(n) for n in ("g_rows", "g_turned", "gt_hi", "gt_lo"))
        r_in, rs_in = sem("r_in"), sem("rs_in")
        sg_out, m_read, m_sum, mt_hi, mt_lo = (sem(n) for n in ("sg_out", "m_read", "m_sum", "mt_hi", "mt_lo"))
        x2_in, x2_out = sem("x2_in"), sem("x2_out")
        h2t_out, h2_stored = sem("h2t_out"), [sem("h2_stored0"), sem("h2_stored1")]
        lt_mm, lt_out, l_turned, l_exp_in, l_exp, sel_ready, rank_mm = (
            sem(n) for n in ("lt_mm", "lt_out", "l_turned", "l_exp_in", "l_exp", "sel_ready", "rank_mm"))
        table_init, pos_ready, table_written, rows_ready, iters_ready = (
            sem(n) for n in ("table_init", "pos_ready", "table_written", "rows_ready", "iters_ready"))
        expert_in = [sem("expert_in0"), sem("expert_in1")]
        gathered = [sem("gathered0"), sem("gathered1")]
        scattered = [sem("scattered0"), sem("scattered1")]
        xg_turned, xt_out_a, xt_out_v = (sem(n) for n in ("xg_turned", "xt_out_a", "xt_out_v"))
        gu_done, silu_done, act_done, act_turned, actt_out, dn_done, y_out_a, y_out_v = (
            sem(n) for n in ("gu_done", "silu_done", "act_done", "act_turned", "actt_out", "dn_done", "y_out_a", "y_out_v"))
        columns = sem("columns")
        pool_passed = sem("pool_passed")
        y_in = [sem(f"y_in{i}") for i in range(NB)]
        out_rows, x3_ready = sem("out_rows"), sem("x3_ready")
        out_stored = sem("out_stored")

        STEP, count = {}, 0
        for u in range(NU):
            for s in range(main_steps(u)):
                count += 1
                STEP[(u, s)] = count

        def gives_result(u):
            return not ((u < 2 or 8 <= u < 16 or u >= 32) and u % 2 == 0)

        def unit_done(u):
            return STEP[(u, main_steps(u) - 1)]

        H_BANKS, G_BANKS = (0, 2, 0, 2, 0), (0, 2, 4, 6, 4)

        block = ctx.enter_context(nc.Block())

        @block.sync
        def _(sp):
            sp.dma_start(CF[:], a["tables"]).then_inc(tables_in, 16)
            for bl in range(NB):
                sp.dma_start(XS[0:rows(bl), bl, :], xrows(bl)).then_inc(x_in[bl], 16)
            sp.dma_start(NMIX[:], a["norm_mix"].partition_broadcast(128).rearrange("p a n -> p (a n)")).then_inc(norm_in, 16)

            def load_unit(u):
                for dst, src in unit_loads(u):
                    sp.dma_start(dst, src).then_inc(raw_in[u % 2], 16)

            def next_unit(u):
                if u >= 2:
                    sp.wait_ge(lo_done, u - 1)
                load_unit(u)

            for u in range(32):
                next_unit(u)
            sp.wait_ge(main_mm, unit_done(30))
            for u in (32, 33):
                next_unit(u)
            for bl in range(NB):
                sp.dma_start(X2[0:rows(bl), bl, :], xrows(bl)).then_inc(x2_in, 16)
            for u in (34, 35):
                next_unit(u)

            def expert_load(u, half, dst_gu, dst_dn, src):
                g, up, dn = src
                for m, w in ((0, g), (1, up)):
                    sp.dma_start(dst_gu[:, half, :, m, :], w.rearrange("(p k) n -> p k n", k=KC)).then_inc(expert_in[u], 16)
                sp.dma_start(dst_dn[:, half, :, :], dn.rearrange("(j p) n -> p j n", p=128)).then_inc(expert_in[u], 16)

            def weights_of(e):
                if isinstance(e, int):
                    return a["w_exp_gate"][0, e], a["w_exp_up"][0, e], a["w_exp_down"][0, e]
                s = bass.ds(e, 1)
                return tuple(a[n][0, s].rearrange("a r n -> (a r) n") for n in ("w_exp_gate", "w_exp_up", "w_exp_down"))

            sp.wait_ge(main_mm, unit_done(31))
            sp.wait_ge(mt_lo, 16)
            for half in range(2):
                expert_load(0, half, WGU[0], WDN[0], weights_of(half))
            sp.wait_ge(main_mm, unit_done(NU - 1))
            sp.dma_start(NFFN[:], a["norm_ffn"].partition_broadcast(128).rearrange("p a n -> p (a n)")).then_inc(norm_in, 16)
            for half in range(2):
                expert_load(1, half, WGU[1], WDN[1], weights_of(2 + half))
            for bl in range(NB):
                sp.wait_ge(h_rows, NB + bl + 1)
                sp.dma_start(h2_d[bl * 128:bl * 128 + rows(bl), :], H2[0:rows(bl), bl % 2, :]).then_inc(h2_stored[bl % 2], 16)
            sp.wait_ge(iters_ready, 2)
            sp.dma_start(NFIN[:], a["norm_final"].partition_broadcast(128)).then_inc(norm_in, 16)
            turns = sp.value_load(ITI[0:1, 0:1], min_val=NFIX // 2, max_val=(NFIX + OVH) // 2)
            with sp.Fori(1, turns) as i:
                for u in range(2):
                    sp.wait_ge(dn_done, 2 * i + u - 1)
                    for half in range(2):
                        e = sp.value_load(ETI[0:1, :, :].rearrange("o p h -> o (p h)")[:, bass.ds(4 * i + 2 * u + half, 1)],
                                          min_val=0, max_val=NE - 1)
                        expert_load(u, half, WGU[u], WDN[u], weights_of(e))
            sp.wait_ge(scattered[0], 16 * turns + 16)
            sp.wait_ge(scattered[1], 16 * turns + 16)
            for bl in range(NB):
                for k in range(2):
                    sp.dma_start(YI[2 * bl + k][0:rows(bl), :],
                                 tok_d[k * NTOK + bl * 128:k * NTOK + bl * 128 + rows(bl), :]).then_inc(y_in[bl], 16)

        @block.gpsimd
        def _(pool):
            for dst, src in ((GN[:], a["gla_norm"].partition_broadcast(128).rearrange("p a n -> p (a n)")),
                             (BG[:], a["b_gla_f"][0].rearrange("(h p) -> p h", p=128)),
                             (SINK[:], a["attn_sinks"].partition_broadcast(128).rearrange("p a n -> p (a n)")),
                             (WR[:, :, 0:NG], a["w_router_group"][0].rearrange("(k p) n -> p k n", p=128)),
                             (WR[:, :, NG:36], a["w_router_expert"][0].rearrange("(k p) n -> p k n", p=128)),
                             (RB[:, 0:NG], a["b_router_group"].partition_broadcast(128).rearrange("p a n -> p (a n)")),
                             (RB[:, NG:36], a["b_router_expert"].partition_broadcast(128).rearrange("p a n -> p (a n)")),
                             (WF2[:], a["w_gla_f2"][0]),
                             (ROWID[:], a["token_rows"])):
                with nc.allow_non_contiguous_dma(reason="a few small parameters"):
                    pool.dma_start(dst, src).then_inc(params_in, 16)
            for m in range(M4):
                with nc.allow_non_contiguous_dma(reason="sinks of the sampled tokens' rows"):
                    pool.dma_start(SINKS[4 * m:4 * m + 4, :],
                                   a["attn_sinks"][0].rearrange("(g m) -> m g", m=M4)[m:m + 1, :].to_broadcast([4, 2])).then_inc(params_in, 16)
            pool.dma_start(slot_d, a["empty_slots"]).then_inc(table_init, 16)
            for name, src in (("sample_win_k", "cache_win_k"), ("sample_win_v", "cache_win_v")):
                pool.dma_start(o[name][0, :, 0:WIN - DS], a[src][0, :, DS:WIN]).then_inc(win_stored, 16)
            pool.wait_ge(h_rows, NB)
            pool.wait_ge(h_turned, NB)
            pool.dma_start(ROPE[:], a["rope"].rearrange("p (a b n) -> p a b n", a=2, b=NB)).then_inc(rope_in, 16)
            pool.dma_start(CK[:], a["cache_win_k"][0].rearrange("b s g d -> s b (g d)")).then_inc(cache_in, 16)
            pool.dma_start(VC[:], a["cache_win_v"][0].rearrange("b s g d -> s b (g d)")).then_inc(cache_in, 16)
            pool.wait_ge(k_roped, NB)
            pool.wait_ge(v_copied, NB)
            pool.dma_start(o["prompt_win_k"][0, 0].rearrange("s g d -> s (g d)"), QK[:, 3, 512:640]).then_inc(kv_stored, 16)
            pool.dma_start(o["prompt_win_v"][0, 0].rearrange("s g d -> s (g d)"), VT[:, 3, :]).then_inc(kv_stored, 16)
            for b in range(DB):
                pool.dma_start(o["sample_win_k"][0, b, WIN - DS:WIN].rearrange("s g d -> s (g d)"),
                               QK[DS * b:DS * b + DS, 4, 512:640]).then_inc(kv_stored, 16)
                pool.dma_start(o["sample_win_v"][0, b, WIN - DS:WIN].rearrange("s g d -> s (g d)"),
                               VT[DS * b:DS * b + DS, 4, :]).then_inc(kv_stored, 16)
            for grp in range(2):
                for bl in range(NB):
                    n = grp * NB + bl
                    pool.wait_ge(r_ready, n + 1)
                    pool.dma_start(rsilu_d[bl, 0:rows(bl), grp * 512:(grp + 1) * 512], RO[0:rows(bl), n % 3, :]).then_inc(r_spilled[n % 3], 16)
            pool.wait_ge(gu_out, 8)
            pool.dma_start(o["prompt_gla_state"][0, 0].rearrange("h k v -> k h v"), ST[:]).then_inc(pstate_stored, 16)
            pool.wait_ge(gd_mm, 8)
            def load_r(bl):
                pool.dma_start(RL[0:rows(bl), :], rsilu_d[bl, 0:rows(bl), :]).then_inc(r_in, 16)

            for h in range(GH):
                buf = (S0, S1)[h % 2]
                if h >= 2:
                    pool.wait_ge(state_stored[h % 2], 16 * (h // 2))
                pool.dma_start(buf[:], a["state_gla"][0, :, h].rearrange("b k v -> k b v")).then_inc(state_in[h % 2], 16)
                if h == 1:
                    for i, n in enumerate((4, 3, 3)):
                        pool.wait_ge(r_spilled[i], 16 * n)
                    load_r(0)
                if h >= 2:
                    pool.wait_ge(g_rows, h - 1)
                    load_r(h - 1)
                if h >= 1:
                    pool.wait_ge(su_out, DB * h)
                    pool.dma_start(o["sample_gla_state"][0, :, h - 1].rearrange("b k v -> k b v"), (S0, S1)[(h - 1) % 2][:]).then_inc(state_stored[(h - 1) % 2], 16)
            pool.wait_ge(g_rows, 3)
            load_r(3)
            pool.wait_ge(so_mm, GH)
            pool.dma_start(RLS[:], rsilu_d[4, 0:32, :]).then_inc(rs_in, 16)
            pool.wait_ge(su_out, DB * GH)
            pool.dma_start(o["sample_gla_state"][0, :, GH - 1].rearrange("b k v -> k b v"), (S0, S1)[(GH - 1) % 2][:]).then_inc(state_stored[(GH - 1) % 2], 16)
            pool.wait_ge(table_init, 16)
            pool.wait_ge(pos_ready, 1)
            for j in range(2 * NB):
                n = rows(j % NB)
                pool.indirect_dma_start(out=slot_d, out_offset=bass.IndirectOffsetOnAxis(ap=POSI[0:n, j:j + 1], axis=0),
                                        in_=ROWID[0:n, j:j + 1], in_offset=None).then_inc(table_written, 16)
            pool.wait_ge(table_written, 16 * 2 * NB)
            for u, (c0, c1) in enumerate(((0, NPC // 2), (NPC // 2, NPC))):
                pool.dma_start(IDXS[:, c0:c1], slot_d.rearrange("(p c) o -> p (c o)", p=128)[:, c0:c1]).then_inc(scattered[u], 16)
            for u in range(2):
                pool.memset(XG[u][:], 0.0).then_inc(columns, 1)
            pool.wait_ge(columns, 2)
            pool.wait_ge(rows_ready, 1)
            pool.wait_ge(h2_stored[0], 48)
            pool.wait_ge(h2_stored[1], 32)

            def gather(u, col):
                pool.indirect_dma_start(out=XG[u][:], out_offset=None, in_=h2_d,
                                        in_offset=bass.IndirectOffsetOnAxis(ap=col[:], axis=0),
                                        bounds_check=NTOK - 1, oob_is_err=False).then_inc(gathered[u], 16)

            pool.tensor_copy(ICG[0][:], IDXG[:, 0:1]).then_inc(columns, 1)
            pool.wait_ge(columns, 3)
            gather(0, ICG[0])
            turns = pool.value_load(ITI[0:1, 0:1], min_val=NFIX // 2, max_val=(NFIX + OVH) // 2)
            with pool.Fori(0, turns) as i:
                for u in range(2):
                    v = 1 - u
                    if u == 0:
                        pool.wait_ge(xg_turned, 2 * i + 1)
                    else:
                        pool.wait_ge(xg_turned, 2 * i + 2)
                    pool.tensor_copy(ICG[v][:], IDXG[:, bass.ds(2 * i + u + 1, 1)]).then_inc(columns, 1)
                    pool.wait_ge(scattered[u], 16 * i + 16)
                    pool.tensor_copy(ICS[u][:], IDXS[:, bass.ds(2 * i + u, 1)]).then_inc(columns, 1)
                    pool.wait_ge(columns, 4 * i + 2 * u + 5)
                    pool.sem_inc(pool_passed, 1)
                    gather(v, ICG[v])
                    pool.wait_ge(y_out_a, 2 * i + u + 2)
                    pool.wait_ge(y_out_v, 2 * i + u + 2)
                    pool.sem_inc(pool_passed, 1)
                    pool.indirect_dma_start(out=tok_d, out_offset=bass.IndirectOffsetOnAxis(ap=ICS[u][:], axis=0),
                                            in_=YO[u][:], in_offset=None,
                                            bounds_check=2 * NTOK - 1, oob_is_err=False).then_inc(scattered[u], 16)
            pool.wait_ge(gathered[0], 16 * turns + 16)
            pool.sem_inc(pool_passed, 1)
            for bl in range(NB):
                pool.wait_ge(out_rows, bl + 1)
                dst = o["y_prompt"][0, bl * 128:(bl + 1) * 128, :] if bl < 4 else o["y_sample"].rearrange("b t d -> (b t) d")
                pool.dma_start(dst, YI[2 * bl][0:rows(bl), :]).then_inc(out_stored, 16)
            pool.wait_ge(out_stored, 16 * NB)
            pool.wait_ge(state_stored[0], 32)
            pool.wait_ge(state_stored[1], 32)
            pool.wait_ge(pstate_stored, 16)
            pool.wait_ge(kv_stored, 16 * (2 + 2 * DB))
            pool.wait_ge(win_stored, 32)

        @block.tensor
        def _(pe):
            mm = nc.tensor.matmul
            HTv = HT[:]

            def three(out, stat, mov, ks, first, last):
                for n, k in enumerate(ks):
                    for m, (x, y) in enumerate(((0, 0), (1, 0), (0, 1))):
                        ins = mm(out, stat(x, k), mov(y, k), start=first and n == 0 and m == 0,
                                 stop=last and n == len(ks) - 1 and m == 2)
                return ins

            def wsplit(u, n):
                return WS[:, u % 2, :, :].rearrange("p x (k n) -> p x k n", n=n)

            def token_step(u, s, act, width, ks0, ks, first, last):
                w = wsplit(u, width)
                return three(P[s][:, 0:width], lambda x, k: act[:, x, ks0 + k, 128 * s:128 * s + 128],
                             lambda y, k: w[:, y, k, :], ks, first, last)

            def column_tile(u, banks, n, c0, w_k0, act, ks):
                w = WS[:, u % 2, :, 0:unit_size(u)].rearrange("p x (k n) -> p x k n", n=n)
                for hf in range(2):
                    ins = three(P[banks[hf]][:, 0:HALF], lambda x, k: w[:, x, w_k0 + k, c0:c0 + 128],
                                lambda y, k: act[:, y, k, HALF * hf:HALF * hf + HALF], ks, True, True)
                return ins

            def main(u, s):
                if s == 0:
                    pe.wait_ge(lo_done, u + 1)
                if u < 2:
                    if (u, s) == (0, 0):
                        pe.wait_ge(h_lo, 2 * NB)
                        pe.wait_ge(memset_done, 1)
                    ins = token_step(u, s, HTv, 512, 4 * u, range(4), u == 0, u == 1)
                elif u == 2:
                    pe.wait_ge(q_roped, s + 1)
                    ins = token_step(u, s, HTv, 256, 0, range(8), True, True)
                elif u == 3:
                    pe.wait_ge(k_roped, 2)
                    pe.wait_ge(v_copied, 2)
                    ins = column_tile(u, (0, 1), 128, 0, 0, HTv, range(8))
                elif u < 8:
                    c = 2 * (u - 4) + s
                    if c < 2:
                        pe.wait_ge(z_out, 4)
                    else:
                        pe.wait_ge(qg_out, 2 * (c - 1))
                    ins = column_tile(u, (2 * (c % 2), 2 * (c % 2) + 1), 256, 128 * s, 0, HTv, range(8))
                elif u < 16:
                    first = u % 2 == 0
                    if u == 8:
                        pe.wait_ge(qg_out, 16)
                    elif u == 10:
                        pe.wait_ge(vg_out, s + 1)
                    elif u == 12:
                        pe.wait_ge(vg_out, NB + s + 1)
                    elif u == 14:
                        pe.wait_ge(r_silu, s + 1)
                    ins = token_step(u, s, HTv, 512, 4 * (u % 2), range(4), first, not first)
                elif u < 32 and u % 2 == 0:
                    j = (u - 16) // 2
                    if j == 0:
                        pe.wait_ge(r_silu, 2 * NB)
                    else:
                        pe.wait_ge(sg_out, 2 * (j - 1) + s + 1)
                    ins = column_tile(u, (2 * s, 2 * s + 1), 256, 128 * s, 0, HTv, range(8))
                elif u < 32:
                    j = (u - 16) // 2
                    if j == 0:
                        pe.wait_ge(gt_lo, 2 * NB)
                        pe.wait_ge(at_lo, 9)
                    else:
                        pe.wait_ge(m_read, 2 * j)
                    column_tile(u, (4, 5), 128, 0, 0, AT[:], range(4))
                    ins = column_tile(u, (6, 7), 128, 0, 4, GT[:], range(8))
                else:
                    first = u % 2 == 0
                    if (u, s) == (32, 0):
                        pe.wait_ge(mt_lo, 16)
                        pe.wait_ge(sg_out, 16)
                    elif u == 34:
                        pe.wait_ge(x2_out, s + 1)
                    ins = token_step(u, s, MT[:], 512, 4 * (u % 2), range(4), first, not first)
                ins.then_inc(main_mm, 1)

            pe.wait_ge(tables_in, 16)
            for bl in range(NB):
                n = rows(bl)
                pe.wait_ge(h_rows, bl + 1)
                if bl >= 2:
                    pe.wait_ge(h_lo, 2 * (bl - 1))
                for k in range(KC):
                    ins = nc.tensor.transpose(P[2 * (bl % 2) + k // 4][:, 128 * (k % 4):128 * (k % 4) + n],
                                              HS[0:n, bl % 2, 128 * k:128 * k + 128], ident[0:n, 0:n])
                ins.then_inc(h_turned, 1)

            def side_pe(step):
                kind, n = step[0], step[1]
                if kind == "T":
                    r = rows(n)
                    pe.wait_ge(k_roped, n + 1)
                    if n:
                        pe.wait_ge(qk_out, 2 * n)
                    for m in range(M4):
                        nc.tensor.transpose(P[5][:, 128 * m:128 * m + r], QK[0:r, n, 128 * m:128 * m + 128], ident[0:r, 0:r])
                    nc.tensor.transpose(P[6][:, 0:r], QK[0:r, n, 512:640], ident[0:r, 0:r]).then_inc(qk_turned, 1)
                elif kind == "CT":
                    pe.wait_ge(cache_in, 32)
                    pe.wait_ge(qk_out, 2 * NB) if n == 0 else pe.wait_ge(ck_out, 1)
                    for b in range(4):
                        ins = nc.tensor.transpose(P[7][:, 128 * b:128 * b + 128], CK[:, 4 * n + b, :], ident)
                    ins.then_inc(ck_turned, 1)
                elif kind == "Z":
                    pe.wait_ge(low_out, 2)
                    pe.wait_ge(params_in, 16 * 13)
                    pe.wait_ge(k_roped, NB)
                    pe.wait_ge(v_copied, NB)
                    for h in range(GH):
                        if h >= 2:
                            pe.wait_ge(z_out, h - 1)
                        for hf in range(2):
                            ins = mm(P[2 * ((h + 1) % 2) + hf][:, 0:HALF], WF2[:, 128 * h:128 * h + 128],
                                     FLT[:, HALF * hf:HALF * hf + HALF], start=True, stop=True)
                        ins.then_inc(z_mm, 1)
                elif kind == "SQ":
                    if n == 0:
                        pe.wait_ge(qk_out, 2 * NB + 1)
                        pe.wait_ge(ck_out, 2)
                    else:
                        pe.wait_ge(sq_out, n)
                    for bi in range(2):
                        b = 2 * n + bi
                        for g in range(2):
                            q = SQT[64 * g:64 * g + 64, b, :]
                            mm(P[5 + g][0:16, 160 * bi:160 * bi + 128], q, CKT[64 * g:64 * g + 64, b, :], start=True, stop=True)
                            ins = mm(P[5 + g][0:16, 160 * bi + 128:160 * bi + 160], q, KT[64 * g:64 * g + 64, NPROMPT:NTOK],
                                     start=True, stop=True)
                    ins.then_inc(sq_mm, 1)
                elif kind == "ST":
                    pe.wait_ge(s_norm, 1)
                    for c in range(16):
                        nc.tensor.transpose(P[5][:, 16 * c:16 * c + 16], SS[:, c, 0:128], ident[0:16, 0:16])
                        ins = nc.tensor.transpose(P[6][0:32, 16 * c:16 * c + 16], SS[:, c, 128:160], ident[0:16, 0:16])
                    ins.then_inc(sp_turned, 1)
                elif kind == "SV":
                    pe.wait_ge(sp_out, 2)
                    for g in range(2):
                        for b in range(DB):
                            c = 2 * b + g
                            out = P[7][64 * g:64 * g + 64, 16 * b:16 * b + 16]
                            mm(out, VC[:, b, 64 * g:64 * g + 64], PTO[:, 16 * c:16 * c + 16], start=True, stop=False)
                            ins = mm(out, VT[0:32, 4, 64 * g:64 * g + 64], PTN[:, 16 * c:16 * c + 16], start=False, stop=True)
                    ins.then_inc(sv_mm, 1)
                elif kind == "QS":
                    bl, g = n // 2, n % 2
                    if n == 0:
                        pe.wait_ge(sp_out, 2)
                    else:
                        pe.wait_ge(sc_out, n)
                    if n >= 2:
                        pe.wait_ge(pt_out, n - 1)
                    k0, kn = (128 * (bl - 1), 256) if bl else (0, 128)
                    for m in range(M4):
                        ins = mm(P[5 + m // 2][:, 256 * (m % 2) + 256 - kn:256 * (m % 2) + 256],
                                 QT[64 * g:64 * g + 64, m, 128 * bl:128 * bl + 128], KT[64 * g:64 * g + 64, k0:k0 + kn],
                                 start=True, stop=True)
                    ins.then_inc(qs_mm, 1)
                elif kind == "QT":
                    bl = n // 2
                    pe.wait_ge(qs_norm, n + 1)
                    pe.wait_ge(sc_out, min(n + 2, 8))
                    for kt in range(0 if bl else 1, 2):
                        for m in range(M4):
                            ins = nc.tensor.transpose(P[5 + kt][:, 128 * m:128 * m + 128], SC[:, n % 2, m, 128 * kt:128 * kt + 128], ident)
                    ins.then_inc(qs_turned, 1)
                elif kind == "QV":
                    bl, g = n // 2, n % 2
                    pe.wait_ge(pt_out, n + 1)
                    pe.wait_ge(at_lo, n + 1)
                    out = P[7][64 * g:64 * g + 64, :]
                    if bl:
                        mm(out, VT[:, bl - 1, 64 * g:64 * g + 64], PT[:, 0, :], start=True, stop=False)
                    mm(out, VT[:, bl, 64 * g:64 * g + 64], PT[:, 1, :], start=not bl, stop=True).then_inc(qv_mm, 1)
                elif kind == "G":
                    st = step[2]
                    if st == 0:
                        pe.wait_ge(kq_ready, n + 1)
                        if n == 0:
                            pe.wait_ge(at_lo, 9)
                        else:
                            pe.wait_ge(go_out, 2 * n)
                        for h in range(GH):
                            for i in range(4):
                                w = 32 * (i + 1)
                                kt = KTL[:, KOFF[i] * GH:(KOFF[i] + w) * GH].rearrange("p (h w) -> p h w", h=GH)
                                ins = mm(P[5][32 * i:32 * i + 32, 128 * h:128 * h + w], QTL[:, h, 32 * i:32 * i + 32], kt[:, h, :],
                                         start=True, stop=True, tile_position=(0, 32 * i))
                        ins.then_inc(ga_mm, 1)
                        pe.wait_ge(b_ready, n + 1)
                        if n:
                            pe.wait_ge(gu_out, 2 * n - 1)
                        for h in range(GH):
                            ins = nc.tensor.transpose(P[6][:, 128 * h:128 * h + 128], KH[:, h, :], ident)
                        ins.then_inc(gk_turned, 1)
                    elif st == 1:
                        pe.wait_ge(ga_out, n + 1)
                        for h in range(GH):
                            ins = nc.tensor.transpose(P[5][:, 128 * h:128 * h + 128], AM[:, h, :], ident)
                        ins.then_inc(gat_turned, 1)
                    elif st in (2, 3):
                        pe.wait_ge(gat_out, n + 1)
                        pe.wait_ge(gk_out, n + 1)
                        if n:
                            pe.wait_ge(gu_out, 2 * n)
                        heads = (0, 1) if st == 2 else (2, 3)
                        obank, ubank = (P[7], P[6]) if st == 2 else (P[5], P[7])
                        for h in heads:
                            out = obank[:, 256 * (h % 2):256 * (h % 2) + 256]
                            mm(out, AMT[:, h, :], VG[:, n, 256 * h:256 * h + 256], start=True, stop=(n == 0))
                            if n:
                                mm(out, QB[:, h, :], ST[:, h, :], start=False, stop=True)
                        if st == 3:
                            pe.wait_ge(go_out, 2 * n + 1)
                        for h in heads:
                            ins = mm(ubank[:, 256 * (h % 2):256 * (h % 2) + 256], KHR[:, h, :], VG[:, n, 256 * h:256 * h + 256],
                                     start=True, stop=True)
                        ins.then_inc(gd_mm, 1)

            def run_units(us):
                for u in us:
                    for s in range(main_steps(u)):
                        main(u, s)
                        for step in side_steps(u, s):
                            side_pe(step)

            run_units(range(16))

            def turn_g(bl):
                n = rows(bl)
                pe.wait_ge(g_rows, bl + 1)
                if bl == 2:
                    pe.wait_ge(so_out, GH)
                    pe.wait_ge(su_out, DB * GH)
                if bl == 4:
                    pe.wait_ge(gt_lo, 2 * 3)
                for k in range(KC):
                    ins = nc.tensor.transpose(P[G_BANKS[bl] + k // 4][:, 128 * (k % 4):128 * (k % 4) + n],
                                              VG[0:n, bl, 128 * k:128 * k + 128], ident[0:n, 0:n])
                ins.then_inc(g_turned, 1)

            pe.wait_ge(s_ready, 1)
            pe.wait_ge(go_out, 8)
            pe.wait_ge(gu_out, 8)
            pe.wait_ge(r_silu, 2 * NB)
            for h in range(GH):
                ins = mm(P[5][0:32, 32 * h:32 * h + 32], SQB[:, h, :], SKT[:, h, :], start=True, stop=True)
            ins.then_inc(sa_mm, 1)
            for h in range(GH):
                ins = nc.tensor.transpose(P[6][0:32, 128 * h:128 * h + 128], SKH[:, h, :], ident)
            ins.then_inc(sk_turned, 1)
            pe.wait_ge(sa_out, 1)
            for h in range(GH):
                ins = nc.tensor.transpose(P[5][0:32, 32 * h:32 * h + 32], AM[0:32, h, 0:32], ident[0:32, 0:32])
            ins.then_inc(sat_turned, 1)
            pe.wait_ge(sat_out, 1)
            pe.wait_ge(sk_out, 1)
            for h in range(GH):
                bank, c = P[6 + h % 2], 0
                if h >= 2:
                    pe.wait_ge(so_out, h - 1)
                pe.wait_ge(state_in[h % 2], 16 * (h // 2 + 1))
                mm(bank[0:32, c:c + 256], AMT[0:32, h, 0:32], VG[0:32, 4, 256 * h:256 * h + 256], start=True, stop=False)
                for b in range(DB):
                    ins = mm(bank[0:32, c:c + 256], SMQ[:, h, b, :], (S0, S1)[h % 2][:, b, :], start=False, stop=(b == DB - 1))
                ins.then_inc(so_mm, 1)
                pe.wait_ge(skm_ready, h + 1)
                for q in range(2):
                    if 2 * h + q:
                        pe.wait_ge(su_out, 4 * (2 * h + q))
                    for b in range(4):
                        ins = mm(P[4 + b // 2][:, 256 * (b % 2):256 * (b % 2) + 256], SKM[:, 4 * q + b, :],
                                 VG[0:32, 4, 256 * h:256 * h + 256], start=True, stop=True)
                    ins.then_inc(su_mm, 1)
                if h >= 2:
                    turn_g(h - 2)
            for bl in (2, 3, 4):
                turn_g(bl)
            run_units(range(16, NU))
            for bl in range(NB):
                n = rows(bl)
                pe.wait_ge(h_rows, NB + bl + 1)
                if bl == 0:
                    pe.wait_ge(x2_out, 2 * NB)
                if bl >= 2:
                    pe.wait_ge(h2t_out, 2 * (bl - 1))
                for k in range(KC):
                    ins = nc.tensor.transpose(P[2 * (bl % 2) + k // 4][:, 128 * (k % 4):128 * (k % 4) + n],
                                              H2[0:n, bl % 2, 128 * k:128 * k + 128], ident[0:n, 0:n])
                ins.then_inc(h_turned, 1)
            pe.wait_ge(h2t_out, 2 * NB)
            for hf in range(2):
                for k in range(KC):
                    ins = mm(P[4 + hf][0:36, 0:HALF], WR[:, k, :], H2T[:, k, HALF * hf:HALF * hf + HALF], start=(k == 0), stop=(k == KC - 1))
            ins.then_inc(lt_mm, 1)
            pe.wait_ge(lt_out, 1)
            for bl in range(NB):
                n = rows(bl)
                ins = nc.tensor.transpose(P[6][0:n, 36 * bl:36 * bl + 36], LT[:, 128 * bl:128 * bl + n], ident[0:36, 0:36])
            ins.then_inc(l_turned, 1)
            pe.wait_ge(sel_ready, 1)
            sel = RR[4][:].rearrange("p b e -> p (b e)")
            mm(P[4][:, 0:160], cst("before"), sel, start=True, stop=True)
            mm(P[5][:, 0:160], cst("ones"), sel, start=True, stop=True).then_inc(rank_mm, 1)
            pe.wait_ge(iters_ready, 2)
            turns = pe.value_load(ITI[0:1, 0:1], min_val=NFIX // 2, max_val=(NFIX + OVH) // 2)

            def turn_rows(u):
                for k in range(KC):
                    ins = nc.tensor.transpose(P[k // 4][:, 128 * (k % 4):128 * (k % 4) + 128],
                                              XG[u][:].rearrange("p (c k) -> p k c", k=KC)[:, k, :], ident)
                ins.then_inc(xg_turned, 1)

            pe.sem_inc(xg_turned, 1)
            pe.sem_inc(act_turned, 1)
            pe.wait_ge(gathered[0], 16)
            turn_rows(0)
            with pe.Fori(0, turns) as i:
                for u in range(2):
                    v = 1 - u
                    n = 2 * i + u
                    pe.wait_ge(expert_in[u], 96 * i + 96)
                    pe.wait_ge(xt_out_a, n + 1)
                    pe.wait_ge(xt_out_v, n + 1)
                    for k in range(KC):
                        for half in range(2):
                            ins = mm(P[2 + u][64 * half:64 * half + 64, :], XT[u][:, k, 64 * half:64 * half + 64],
                                     WGU[u][:, half, k, :, :].rearrange("p m n -> p (m n)"), start=(k == 0), stop=(k == KC - 1))
                    ins.then_inc(gu_done, 1)
                    pe.wait_ge(gathered[v], 16 * i + (16 if u == 0 else 32))
                    turn_rows(v)
                    pe.wait_ge(act_done, n + 2)
                    for j in range(2):
                        ins = nc.tensor.transpose(P[4 + u][:, 128 * j:128 * j + 128], AC[u][:, 128 * j:128 * j + 128], ident)
                    ins.then_inc(act_turned, 1)
                    pe.wait_ge(actt_out, n + 1)
                    pe.wait_ge(y_out_a, n + 1)
                    pe.wait_ge(y_out_v, n + 1)
                    for c in range(2):
                        for j in range(2):
                            for half in range(2):
                                ins = mm(P[6 + c][64 * half:64 * half + 64, :], ACTT[u][:, j, 64 * half:64 * half + 64],
                                         WDN[u][:, half, j, 512 * c:512 * c + 512], start=(j == 0), stop=(j == 1))
                    ins.then_inc(dn_done, 1)

        @block.scalar
        def _(act):
            A = nc.scalar.activation
            act.wait_ge(memset_done, 1)
            for bl in range(NB):
                act.wait_ge(x_in[bl], 16)
                if bl:
                    act.wait_ge(squares, bl)
                A(JUNK[0:rows(bl), :], XS[0:rows(bl), bl, :], ACT.Square, accum_out=SSQ[0:rows(bl), bl:bl + 1]).then_inc(squares, 1)
            act.wait_ge(variance, 1)
            A(RST[:], SSQ[:], ACT.Sqrt).then_inc(root, 1)

            def split_hi(u):
                act.wait_ge(raw_in[u % 2], unit_full[u])
                if u >= 2:
                    act.wait_ge(main_mm, unit_done(u - 2))
                    act.wait_ge(lo_done, u - 1)
                n = unit_size(u)
                A(WS[:, u % 2, 0, 0:n], RAW[:, u % 2, 0:n], ACT.Copy).then_inc(hi_done, 1)

            split_hi(0)
            split_hi(1)
            for bl in range(NB):
                n = rows(bl)
                act.wait_ge(h_turned, bl + 1)
                for q in range(2):
                    A(HT[:, 0, 4 * q:4 * q + 4, 128 * bl:128 * bl + n],
                      P[2 * (bl % 2) + q][:].rearrange("p (k n) -> p k n", k=4)[:, :, 0:n], ACT.Copy).then_inc(h_hi, 1)

            def main(u, s):
                if not gives_result(u):
                    return
                act.wait_ge(main_mm, STEP[(u, s)])
                n = rows(s)
                if u == 2:
                    act.wait_ge(k_roped, s + 1)
                    A(VT[0:n, s, :], P[s][0:n, 128:256], ACT.Copy).then_inc(v_copied, 1)
                elif u == 3:
                    act.wait_ge(k_roped, NB)
                    for hf in range(2):
                        A(FLT[:, HALF * hf:HALF * hf + HALF], P[hf][0:16, 0:HALF], ACT.Copy).then_inc(low_out, 1)
                elif 4 <= u < 8:
                    c = 2 * (u - 4) + s
                    for hf in range(2):
                        A(QKG[:, c, HALF * hf:HALF * hf + HALF], P[2 * (c % 2) + hf][:, 0:HALF], ACT.Copy,
                          scale=float(DK) ** -0.5 if c < 4 else 1.0).then_inc(qg_out, 1)
                elif u in (9, 11):
                    grp = (u - 9) // 2
                    if (u, s) == (9, 0):
                        act.wait_ge(sp_turned, 1)
                        act.wait_ge(sv_mm, 1)
                    A(VG[0:n, s, 512 * grp:512 * grp + 512], P[s][0:n, :], ACT.Copy).then_inc(vg_out, 1)
                elif u in (13, 15):
                    q = (u - 13) // 2 * NB + s
                    if q >= 3:
                        act.wait_ge(r_spilled[q % 3], 16 * (q // 3))
                    if q == 0:
                        act.wait_ge(qv_mm, 8)
                    A(RO[0:n, q % 3, :], P[s][0:n, :], ACT.Silu).then_inc(r_silu, 1)
                elif 16 <= u < 32 and u % 2 == 0:
                    j = (u - 16) // 2
                    if j >= 2:
                        act.wait_ge(m_read, 2 * (j - 1))
                    if u == 16:
                        act.wait_ge(state_stored[0], 32)
                        act.wait_ge(state_stored[1], 32)
                    for hf in range(2):
                        ins = A(SG[:, j % 2, s, HALF * hf:HALF * hf + HALF], P[2 * s + hf][:, 0:HALF], ACT.Sigmoid)
                    ins.then_inc(sg_out, 1)
                elif 16 <= u < 32:
                    j = (u - 16) // 2
                    act.wait_ge(m_sum, j + 1)
                    A(MT[:, 0, j, 0:NTOK], MTMP[:, 0, :], ACT.Copy).then_inc(mt_hi, 1)
                elif u in (33, 35):
                    grp = (u - 33) // 2
                    act.wait_ge(mt_lo, 16)
                    act.wait_ge(x2_out, NB * grp + s + 1)
                    act.wait_ge(squares, NB + NB * grp + s)
                    A(P[5 + grp][0:n, :], X2[0:n, s, 512 * grp:512 * grp + 512], ACT.Square,
                      accum_out=SSH[0:n, grp, s:s + 1]).then_inc(squares, 1)

            def side_act(step):
                kind, n = step[0], step[1]
                if kind == "T":
                    r = rows(n)
                    act.wait_ge(qk_turned, n + 1)
                    A(QT[:, :, 128 * n:128 * n + r], P[5][:].rearrange("p (m t) -> p m t", m=4)[:, :, 0:r], ACT.Copy,
                      scale=float(HD) ** -0.5).then_inc(qk_out, 1)
                    A(KT[:, 128 * n:128 * n + r], P[6][:, 0:r], ACT.Copy).then_inc(qk_out, 1)
                    if n == 4:
                        act.wait_ge(qk_out, 2 * NB)
                        A(SQT[:].rearrange("p b (m t) -> p b m t", m=4), QT[:, :, NPROMPT:NTOK].rearrange("p m (b t) -> p b m t", t=DS),
                          ACT.Copy).then_inc(qk_out, 1)
                elif kind == "CT":
                    act.wait_ge(ck_turned, n + 1)
                    A(CKT[:, 4 * n:4 * n + 4, :], P[7][:].rearrange("p (b t) -> p b t", b=4), ACT.Copy).then_inc(ck_out, 1)
                elif kind == "Z":
                    act.wait_ge(z_out, GH)
                    A(ZT[:], LA[:], ACT.Abs).then_inc(z_abs, 1)
                    act.wait_ge(z_abs, 1)
                    A(ZT[:], ZT[:], ACT.Exp, scale=-1.0).then_inc(z_abs, 1)
                    act.wait_ge(z_abs, 2)
                    A(ZT[:], ZT[:], ACT.Ln, bias=1.0).then_inc(z_ln, 1)
                elif kind == "SQ" and n == 3:
                    act.wait_ge(s_exp_in, 1)
                    A(SS[:], SS[:], ACT.Exp).then_inc(s_exp, 1)
                    A(SSK[:], SSK[:], ACT.Exp).then_inc(s_exp, 1)
                elif kind == "ST":
                    act.wait_ge(sp_turned, 1)
                    A(PTO[:], P[5][:, 0:256], ACT.Copy).then_inc(sp_out, 1)
                    A(PTN[:], P[6][0:32, 0:256], ACT.Copy).then_inc(sp_out, 1)
                elif kind == "SV":
                    act.wait_ge(sv_mm, 1)
                    for b in range(1):
                        A(AT[:, 0, :, NPROMPT:NTOK].rearrange("p m (b t) -> p b m t", t=DS),
                          P[7][:, 0:128].rearrange("p (b m t) -> p b m t", b=DB, m=M4), ACT.Copy).then_inc(at_hi, 1)
                elif kind == "QS":
                    act.wait_ge(qs_max, n + 1)
                    w = n % 2
                    k0 = 0 if n >= 2 else 128
                    for m in range(M4):
                        A(SC[:, w, m, k0:256], SC[:, w, m, k0:256], ACT.Exp, bias=NMX[:, w, m:m + 1], accum_out=SUM[:, w, m:m + 1])
                    A(ESK[:, w, :], ESK[:, w, :], ACT.Exp).then_inc(qs_exp, 1)
                elif kind == "QT":
                    act.wait_ge(qs_turned, n + 1)
                    if n >= 1:
                        act.wait_ge(qv_mm, n)
                    for kt in range(0 if n >= 2 else 1, 2):
                        ins = A(PT[:, kt, :], P[5 + kt][:], ACT.Copy)
                    ins.then_inc(pt_out, 1)
                elif kind == "QV":
                    bl, g = n // 2, n % 2
                    act.wait_ge(qv_mm, n + 1)
                    A(AT[64 * g:64 * g + 64, 0, :, 128 * bl:128 * bl + 128],
                      P[7][64 * g:64 * g + 64, :].rearrange("p (m t) -> p m t", m=4), ACT.Copy).then_inc(at_hi, 1)
                elif kind == "GP" or (kind == "G" and step[2] == 1 and n < 3):
                    c = n if kind == "GP" else n + 1
                    act.wait_ge(k_arg, c + 1)
                    A(KD[:], KD[:], ACT.Exp, scale=1.0 / 16)
                    A(QD[:], QD[:], ACT.Exp, scale=1.0 / 16).then_inc(k_exp, 1)
                    if kind == "GP":
                        exp_b(0)
                if kind == "G":
                    st = step[2]
                    if st == 0:
                        act.wait_ge(gk_turned, n + 1)
                        A(KHR[:], P[6][:].rearrange("p (h t) -> p h t", h=GH), ACT.Copy).then_inc(gk_out, 1)
                    elif st == 1:
                        act.wait_ge(gat_turned, n + 1)
                        A(AMT[:], P[5][:].rearrange("p (h t) -> p h t", h=GH), ACT.Copy).then_inc(gat_out, 1)
                    elif st in (2, 3):
                        act.wait_ge(gd_mm, 2 * n + st - 1)
                        bank = P[7] if st == 2 else P[5]
                        for hh in range(2):
                            square_o(bank[:, 256 * hh:256 * hh + 256], n, 2 * (st - 2) + hh)
                        A(VG[:, n, 512 * (st - 2):512 * (st - 2) + 512], bank[:], ACT.Copy).then_inc(go_out, 1)
                    elif n < 3:
                        exp_b(n + 1)

            o_count = [0]

            def square_o(src, bl, h):
                act.wait_ge(o_squares, o_count[0])
                o_count[0] += 1
                r = rows(bl)
                A(OJ[0:r, :], src, ACT.Square, accum_out=OSQ[0:r, bl, h:h + 1]).then_inc(o_squares, 1)

            def exp_b(c):
                act.wait_ge(b_arg, c + 1)
                if c:
                    act.wait_ge(gd_mm, 2 * c)
                    act.wait_ge(gu_out, 2 * c)
                A(QB[:], LA[:, :, 128 * c:128 * c + 128], ACT.Exp, scale=1.0 / 16)
                A(EBL[:], LA[:, :, 128 * c + 127], ACT.Exp, scale=1.0 / 16)
                A(KH[:], KH[:], ACT.Exp, scale=1.0 / 16).then_inc(b_exp, 1)

            def run_units(us):
                for u in us:
                    for s in range(main_steps(u)):
                        main(u, s)
                        for step in side_steps(u, s):
                            side_act(step)
                    if u + 2 < NU:
                        split_hi(u + 2)

            run_units(range(16))
            act.wait_ge(s_arg, 1)
            A(SQB[:], LA[:, :, NPROMPT:NTOK], ACT.Exp, scale=1.0 / 16)
            A(SKT[:], LA[:, :, NPROMPT:NTOK], ACT.Exp, scale=-1.0 / 16)
            A(SEBL[:], LA[:, :, NPROMPT + DS - 1:NTOK:DS], ACT.Exp, scale=1.0 / 16)
            A(SKH[:], SKH[:], ACT.Exp, scale=1.0 / 16).then_inc(s_exps, 1)
            act.wait_ge(sk_turned, 1)
            A(KHR[0:32], P[6][0:32, :].rearrange("p (h t) -> p h t", h=GH), ACT.Copy).then_inc(sk_out, 1)
            act.wait_ge(sat_turned, 1)
            A(AMT[0:32, :, 0:32], P[5][0:32, 0:128].rearrange("p (h t) -> p h t", h=GH), ACT.Copy).then_inc(sat_out, 1)
            act.wait_ge(variance, 2)
            A(ORS[:, 0:4], OSQ[:, 0:4], ACT.Sqrt).then_inc(root, 1)

            def gt_upper(bl):
                n = rows(bl)
                act.wait_ge(g_turned, bl + 1)
                for q in range(2):
                    A(GT[:, 0, 4 * q:4 * q + 4, 128 * bl:128 * bl + n],
                      P[G_BANKS[bl] + q][:].rearrange("p (k n) -> p k n", k=4)[:, :, 0:n], ACT.Copy).then_inc(gt_hi, 1)

            act.wait_ge(s_ready, 1)
            for h in range(GH):
                act.wait_ge(su_mm, 2 * h + 2)
                src = P[6 + h % 2][0:32, 0:256]
                square_o(src, 4, h)
                A(VG[0:32, 4, 256 * h:256 * h + 256], src, ACT.Copy).then_inc(so_out, 1)
                if h >= 2:
                    gt_upper(h - 2)
            act.wait_ge(variance, 3)
            A(ORS[:, 4:5], OSQ[:, 4:5], ACT.Sqrt).then_inc(root, 1)
            for bl in (2, 3, 4):
                gt_upper(bl)
            run_units(range(16, NU))
            act.wait_ge(variance, 4)
            A(RST[:], SSQ[:], ACT.Sqrt).then_inc(root, 1)
            for bl in range(NB):
                n = rows(bl)
                act.wait_ge(h_turned, NB + bl + 1)
                for q in range(2):
                    A(H2T[:, 4 * q:4 * q + 4, 128 * bl:128 * bl + n],
                      P[2 * (bl % 2) + q][:].rearrange("p (k n) -> p k n", k=4)[:, :, 0:n], ACT.Copy).then_inc(h2t_out, 1)
            act.wait_ge(lt_mm, 1)
            for hf in range(2):
                ins = A(LT[:, HALF * hf:HALF * hf + HALF], P[4 + hf][0:36, 0:HALF], ACT.Copy)
            ins.then_inc(lt_out, 1)
            act.wait_ge(l_exp_in, 1)
            A(RG[2][:], RG[2][:], ACT.Exp).then_inc(l_exp, 1)
            act.wait_ge(l_exp_in, 2)
            A(R1["e2"][:], R1["d"][:], ACT.Exp).then_inc(l_exp, 1)
            act.wait_ge(iters_ready, 2)
            turns = act.value_load(ITI[0:1, 0:1], min_val=NFIX // 2, max_val=(NFIX + OVH) // 2)

            def xt_half(u):
                A(XT[u][:, 0:4, :], P[0][:].rearrange("p (k n) -> p k n", k=4), ACT.Copy).then_inc(xt_out_a, 1)

            act.sem_inc(y_out_a, 1)
            act.wait_ge(xg_turned, 2)
            xt_half(0)
            with act.Fori(0, turns) as i:
                for u in range(2):
                    n = 2 * i + u
                    act.wait_ge(gu_done, n + 1)
                    act.wait_ge(act_done, n + 1)
                    A(SA[:], P[2 + u][:, 0:FF], ACT.Silu).then_inc(silu_done, 1)
                    act.wait_ge(xg_turned, n + 3)
                    xt_half(1 - u)
                    act.wait_ge(dn_done, n + 1)
                    act.wait_ge(scattered[u], 16 * i + 16)
                    A(YO[u][:, 0:512], P[6][:], ACT.Copy).then_inc(y_out_a, 1)
            for bl in range(NB):
                act.wait_ge(x3_ready, bl + 1)
                act.wait_ge(squares, 3 * NB + bl)
                A(JUNK3[0:rows(bl), :], YI[2 * bl][0:rows(bl), :], ACT.Square, accum_out=SSQ[0:rows(bl), bl:bl + 1]).then_inc(squares, 1)
                act.wait_ge(variance, 4 + bl + 1)
                A(RST[:, bl:bl + 1], SSQ[:, bl:bl + 1], ACT.Sqrt).then_inc(root, 1)

        @block.vector
        def _(dve):
            V = nc.vector
            chain = [0]

            def link(ins):
                chain[0] += 1
                ins.then_inc(dve_step, 1)
                dve.wait_ge(dve_step, chain[0])

            V.memset(SSQ[:], 1.0)
            V.memset(SSH[:], 1.0)
            V.memset(OSQ[:], 1.0)
            V.memset(HT[:, :, :, NTOK:PADTOK].bitcast(F), 0.0).then_inc(memset_done, 1)
            dve.wait_ge(squares, NB)
            V.tensor_scalar(SSQ[:], SSQ[:], 1.0 / D, EPS, ALU.mult, ALU.add).then_inc(variance, 1)
            dve.wait_ge(root, 1)
            link(V.reciprocal(RST[:], RST[:]))
            dve.wait_ge(norm_in, 16)

            def lower_part(dst, banks, bl, upper, done):
                n = rows(bl)
                for q in range(2):
                    dve.wait_ge(upper, 2 * bl + q + 1)
                    c = slice(128 * bl, 128 * bl + n)
                    V.tensor_tensor(dst[:, 1, 4 * q:4 * q + 4, c], P[banks[bl] + q][:].rearrange("p (k n) -> p k n", k=4)[:, :, 0:n],
                                    dst[:, 0, 4 * q:4 * q + 4, c].bitcast(F), ALU.subtract).then_inc(done, 1)

            def ht_lo(bl):
                lower_part(HT, H_BANKS, bl, h_hi, h_lo)

            for bl in range(NB):
                n = rows(bl)
                if bl >= 2:
                    dve.wait_ge(h_turned, bl - 1)
                V.scalar_tensor_tensor(out=HS[0:n, bl % 2, :], in0=XS[0:n, bl, :], scalar=RST[0:n, bl:bl + 1],
                                       in1=NMIX[0:n, :], op0=ALU.mult, op1=ALU.mult).then_inc(h_rows, 1)
                if bl >= 1:
                    ht_lo(bl - 1)
            ht_lo(NB - 1)

            def split_lo(u):
                dve.wait_ge(hi_done, u + 1)
                n = unit_size(u)
                V.tensor_tensor(WS[:, u % 2, 1, 0:n], RAW[:, u % 2, 0:n], WS[:, u % 2, 0, 0:n].bitcast(F), ALU.subtract).then_inc(lo_done, 1)

            split_lo(0)
            split_lo(1)

            def rotate(bl, nh, src, dst):
                n = rows(bl)
                x = src.rearrange("p (h d) -> p h d", d=64)
                cos = ROPE[0:n, 0, bl, :].unsqueeze(1).to_broadcast([n, nh, 64])
                sin = ROPE[0:n, 1, bl, :]
                a1 = RT[0:n, 0, 0:64 * nh].rearrange("p (h d) -> p h d", d=64)
                a2 = RT[0:n, 1, 0:64 * nh].rearrange("p (h d) -> p h d", d=64)
                V.tensor_tensor(a1, x, cos, ALU.mult)
                V.tensor_tensor(a2[:, :, 0:32], x[:, :, 32:64], sin[:, 0:32].unsqueeze(1).to_broadcast([n, nh, 32]), ALU.mult)
                link(V.tensor_tensor(a2[:, :, 32:64], x[:, :, 0:32], sin[:, 32:64].unsqueeze(1).to_broadcast([n, nh, 32]), ALU.mult))
                if nh == AH:
                    a1 = a1.rearrange("p (g m) d -> p g m d", g=2)
                    a2 = a2.rearrange("p (g m) d -> p g m d", g=2)
                return V.tensor_tensor(dst, a1, a2, ALU.add)

            def main(u, s):
                if not gives_result(u):
                    return
                n = rows(s)
                if u in (1, 2):
                    dve.wait_ge(main_mm, STEP[(u, s)])
                if u == 1:
                    if s == 0:
                        dve.wait_ge(rope_in, 16)
                    rotate(s, AH, P[s][0:n, :], QK[0:n, s, 0:512].rearrange("p (m g d) -> p g m d", m=4, g=2)).then_inc(q_roped, 1)
                    dve.wait_ge(q_roped, s + 1)
                elif u == 2:
                    rotate(s, KVH, P[s][0:n, 0:128], QK[0:n, s, 512:640].rearrange("p (h d) -> p h d", d=64)).then_inc(k_roped, 1)
                    dve.wait_ge(k_roped, s + 1)
                elif u in (13, 15):
                    q = (u - 13) // 2 * NB + s
                    dve.wait_ge(r_silu, q + 1)
                    r = RO[0:n, q % 3, :].rearrange("p (h v) -> p h v", h=2)
                    V.tensor_tensor(r, r, GN[0:n, :].unsqueeze(1).to_broadcast([n, 2, DV]), ALU.mult).then_inc(r_ready, 1)
                elif 16 <= u < 32 and u % 2:
                    j = (u - 16) // 2
                    dve.wait_ge(main_mm, STEP[(u, s)])
                    dve.wait_ge(sg_out, 2 * j + 2)
                    if j:
                        dve.wait_ge(mt_hi, j)
                        dve.wait_ge(mt_lo, 2 * j)
                    for br in range(2):
                        for hf in range(2):
                            ins = V.tensor_tensor(MTMP[:, br, HALF * hf:HALF * hf + HALF], P[4 + 2 * br + hf][:, 0:HALF],
                                                  SG[:, j % 2, br, HALF * hf:HALF * hf + HALF], ALU.mult)
                        ins.then_inc(m_read, 1)
                    dve.wait_ge(m_read, 2 * j + 2)
                    V.tensor_tensor(MTMP[:, 0, :], MTMP[:, 0, :], MTMP[:, 1, :], ALU.add).then_inc(m_sum, 1)
                    dve.wait_ge(m_sum, j + 1)
                    dve.wait_ge(mt_hi, j + 1)
                    V.tensor_tensor(MT[:, 1, j, 0:NTOK], MTMP[:, 0, :], MT[:, 0, j, 0:NTOK].bitcast(F), ALU.subtract).then_inc(mt_lo, 2)
                elif u in (33, 35):
                    grp = (u - 33) // 2
                    dve.wait_ge(main_mm, STEP[(u, s)])
                    if (u, s) == (33, 0):
                        dve.wait_ge(x2_in, 16 * NB)
                    x = X2[0:n, s, 512 * grp:512 * grp + 512]
                    V.tensor_tensor(x, x, P[s][0:n, :], ALU.add).then_inc(x2_out, 1)

            def side_dve(step):
                kind, n = step[0], step[1]
                if kind == "Z":
                    for h in range(GH):
                        dve.wait_ge(z_mm, h + 1)
                        for hf in range(2):
                            ins = V.tensor_scalar(LA[:, h, HALF * hf:HALF * hf + HALF], P[2 * ((h + 1) % 2) + hf][:, 0:HALF],
                                                  BG[:, h:h + 1], None, ALU.add)
                        ins.then_inc(z_out, 1)
                    dve.wait_ge(z_out, GH)
                    dve.wait_ge(z_ln, 1)
                    link(V.scalar_tensor_tensor(out=LA[:], in0=LA[:], scalar=0.0, in1=ZT[:], op0=ALU.min, op1=ALU.subtract))
                    for h in range(GH):
                        ins = V.tensor_tensor_scan(out=ZT[:, h, :], data0=cst("scan"), data1=LA[:, h, :], initial=0.0,
                                                   op0=ALU.mult, op1=ALU.add)
                    link(ins)
                    V.tensor_copy(LA[:], ZT[:]).then_inc(decay_ready, 1)
                elif kind == "SQ":
                    dve.wait_ge(sq_mm, n + 1)
                    for g in range(2):
                        sc = SS[:].rearrange("p (b g) k -> p g b k", g=2)[:, g, 2 * n:2 * n + 2, :]
                        ps = P[5 + g][0:16, 0:320].rearrange("p (b k) -> p b k", b=2)
                        V.tensor_tensor(sc[:, :, 0:128], ps[:, :, 0:128], cst("s_old")[0:16].unsqueeze(1).to_broadcast([16, 2, 128]), ALU.add)
                        ins = V.tensor_tensor(sc[:, :, 128:160], ps[:, :, 128:160],
                                              cst("s_new")[0:16].rearrange("p (b k) -> p b k", b=DB)[:, 2 * n:2 * n + 2, :], ALU.add)
                    ins.then_inc(sq_out, 1)
                    if n == 3:
                        dve.wait_ge(sq_out, 4)
                        link(V.tensor_reduce(SMX[:], SS[:], axis=AX.X, op=ALU.max))
                        sk = SINKS[:].unsqueeze(1).to_broadcast([16, DB, 2])
                        mx = SMX[:].rearrange("p (b g) -> p b g", g=2)
                        link(V.tensor_tensor(mx, mx, sk, ALU.max))
                        V.tensor_tensor(SSK[:].rearrange("p (b g) -> p b g", g=2), sk, mx, ALU.subtract)
                        V.tensor_tensor(SS[:], SS[:], SMX[:].unsqueeze(2).to_broadcast([16, 16, 160]), ALU.subtract).then_inc(s_exp_in, 1)
                        dve.wait_ge(s_exp, 2)
                        link(V.tensor_reduce(SSM[:], SS[:], axis=AX.X, op=ALU.add))
                        link(V.tensor_tensor(SSM[:], SSM[:], SSK[:], ALU.add))
                        link(V.reciprocal(SSM[:], SSM[:]))
                        V.tensor_tensor(SS[:], SS[:], SSM[:].unsqueeze(2).to_broadcast([16, 16, 160]), ALU.mult).then_inc(s_norm, 1)
                elif kind == "SV":
                    dve.wait_ge(at_hi, 1)
                    hi = AT[:, 0, :, NPROMPT:NTOK].bitcast(F).rearrange("p m (b t) -> p b m t", t=DS)
                    lo = AT[:, 1, :, NPROMPT:NTOK].rearrange("p m (b t) -> p b m t", t=DS)
                    V.tensor_tensor(lo, P[7][:, 0:128].rearrange("p (b m t) -> p b m t", b=DB, m=M4), hi, ALU.subtract).then_inc(at_lo, 1)
                elif kind == "QS":
                    w, g = n % 2, n % 2
                    k0 = 0 if n >= 2 else 128
                    dve.wait_ge(qs_mm, n + 1)
                    if n == 0:
                        dve.wait_ge(kv_stored, 16 * (2 + 2 * DB))
                    if n >= 2:
                        dve.wait_ge(qs_turned, n - 1)
                    for q in range(2):
                        ins = V.tensor_tensor(SC[:, w, 2 * q:2 * q + 2, k0:256],
                                              P[5 + q][:].rearrange("p (m k) -> p m k", m=2)[:, :, k0:256],
                                              cst("window")[:, k0:256].unsqueeze(1).to_broadcast([128, 2, 256 - k0]), ALU.add)
                    ins.then_inc(sc_out, 1)
                    dve.wait_ge(sc_out, n + 1)
                    link(V.tensor_reduce(MX[:, w, :], SC[:, w, :, k0:256], axis=AX.X, op=ALU.max))
                    sk = SINK[:, 4 * g:4 * g + 4]
                    link(V.tensor_tensor(MX[:, w, :], MX[:, w, :], sk, ALU.max))
                    V.tensor_tensor(ESK[:, w, :], sk, MX[:, w, :], ALU.subtract)
                    V.tensor_scalar(NMX[:, w, :], MX[:, w, :], -1.0, None, ALU.mult).then_inc(qs_max, 1)
                    dve.wait_ge(qs_exp, n + 1)
                    link(V.tensor_tensor(DEN[:, w, :], SUM[:, w, :], ESK[:, w, :], ALU.add))
                    link(V.reciprocal(DEN[:, w, :], DEN[:, w, :]))
                    V.tensor_tensor(SC[:, w, :, k0:256], SC[:, w, :, k0:256],
                                    DEN[:, w, :].unsqueeze(2).to_broadcast([128, 4, 256 - k0]), ALU.mult).then_inc(qs_norm, 1)
                elif kind == "QV":
                    bl, g = n // 2, n % 2
                    dve.wait_ge(at_hi, n + 2)
                    V.tensor_tensor(AT[64 * g:64 * g + 64, 1, :, 128 * bl:128 * bl + 128],
                                    P[7][64 * g:64 * g + 64, :].rearrange("p (m t) -> p m t", m=4),
                                    AT[64 * g:64 * g + 64, 0, :, 128 * bl:128 * bl + 128].bitcast(F), ALU.subtract).then_inc(at_lo, 1)
                elif kind == "GP":
                    dve.wait_ge(qg_out, 16)
                    dve.wait_ge(decay_ready, 1)
                    dve.wait_ge(qv_mm, 8)
                    link(V.memset(AM[:], 0.0))
                    decays_arg(0)
                    to_end_arg(0)
                    decays_use(0)
                    to_end_use(0)
                elif kind == "G":
                    st = step[2]
                    if st == 0:
                        dve.wait_ge(ga_mm, n + 1)
                        if n:
                            dve.wait_ge(gat_turned, n)
                        for i in range(4):
                            w = 32 * (i + 1)
                            pr = slice(32 * i, 32 * i + 32)
                            ins = V.tensor_tensor(AM[pr, :, 0:w], P[5][pr, :].rearrange("p (h s) -> p h s", h=GH)[:, :, 0:w],
                                                  cst("causal")[pr, 0:w].unsqueeze(1).to_broadcast([32, GH, w]), ALU.mult)
                        ins.then_inc(ga_out, 1)
                    elif st == 1:
                        if n < 3:
                            decays_arg(n + 1)
                            decays_use(n + 1)
                    elif st in (2, 3):
                        dve.wait_ge(gd_mm, 2 * n + st - 1)
                        bank = P[6] if st == 2 else P[7]
                        for hh in range(2):
                            h = 2 * (st - 2) + hh
                            src = bank[:, 256 * hh:256 * hh + 256]
                            if n == 0:
                                ins = V.tensor_copy(ST[:, h, :], src)
                            else:
                                ins = V.scalar_tensor_tensor(out=ST[:, h, :], in0=ST[:, h, :], scalar=EBL[:, h:h + 1], in1=src,
                                                             op0=ALU.mult, op1=ALU.add)
                        ins.then_inc(gu_out, 1)
                    elif n < 3:
                        to_end_arg(n + 1)
                        to_end_use(n + 1)

            def k_ref(c, i):
                return LA[:, :, 128 * c + 32 * i + 15]

            def decays_arg(c):
                if c:
                    dve.wait_ge(ga_mm, c)
                b = LA[:, :, 128 * c:128 * c + 128]
                for i in range(4):
                    w = 32 * (i + 1)
                    kd = KD[:, KOFF[i] * GH:(KOFF[i] + w) * GH].rearrange("p (h w) -> p h w", h=GH)
                    V.tensor_tensor(kd, k_ref(c, i).unsqueeze(2).to_broadcast([128, GH, w]), b[:, :, 0:w], ALU.subtract)
                bq = b.rearrange("p h (i t) -> p h i t", i=4)
                V.tensor_tensor(QD[:].rearrange("p h (i t) -> p h i t", i=4), bq,
                                bq[:, :, :, 15:16].to_broadcast([128, GH, 4, 32]), ALU.subtract).then_inc(k_arg, 1)

            def decays_use(c):
                dve.wait_ge(k_exp, c + 1)
                for i in range(4):
                    w = 32 * (i + 1)
                    kv = [t[:, KOFF[i] * GH:(KOFF[i] + w) * GH].rearrange("p (h w) -> p h w", h=GH) for t in (KTL, KD)]
                    V.tensor_tensor(kv[0], kv[1], QKG[:, 4:8, 128 * c:128 * c + w], ALU.mult)
                V.tensor_tensor(QTL[:], QD[:], QKG[:, 0:4, 128 * c:128 * c + 128], ALU.mult).then_inc(kq_ready, 1)

            def to_end_arg(c):
                b = LA[:, :, 128 * c:128 * c + 128]
                V.tensor_tensor(KH[:], b[:, :, 127:128].to_broadcast([128, GH, 128]), b, ALU.subtract).then_inc(b_arg, 1)

            def to_end_use(c):
                dve.wait_ge(b_exp, c + 1)
                V.tensor_tensor(KH[:], KH[:], QKG[:, 4:8, 128 * c:128 * c + 128], ALU.mult)
                V.tensor_tensor(QB[:], QB[:], QKG[:, 0:4, 128 * c:128 * c + 128], ALU.mult).then_inc(b_ready, 1)

            def run_units(us):
                for u in us:
                    for s in range(main_steps(u)):
                        main(u, s)
                        for step in side_steps(u, s):
                            side_dve(step)
                    if u + 2 < NU:
                        split_lo(u + 2)

            run_units(range(16))

            dve.wait_ge(gd_mm, 8)
            b4 = LA[:, :, NPROMPT:NTOK].rearrange("p h (b t) -> p h b t", t=DS)
            V.tensor_tensor(SKH[:].rearrange("p h (b t) -> p h b t", t=DS), b4[:, :, :, DS - 1:DS].to_broadcast([128, GH, DB, DS]),
                            b4, ALU.subtract).then_inc(s_arg, 1)
            dve.wait_ge(s_exps, 1)
            q4, k4 = QKG[:, 0:4, NPROMPT:NTOK], QKG[:, 4:8, NPROMPT:NTOK]
            V.tensor_tensor(SKT[:], SKT[:], k4, ALU.mult)
            V.tensor_tensor(SKH[:], SKH[:], k4, ALU.mult)
            link(V.tensor_tensor(SQB[:], SQB[:], q4, ALU.mult))
            dve.wait_ge(pstate_stored, 16)
            V.tensor_tensor(SMQ[:], SQB[:].unsqueeze(2).to_broadcast([128, GH, DB, 32]),
                            cst("of_batch").rearrange("p (b t) -> p b t", b=DB).unsqueeze(1).to_broadcast([128, GH, DB, 32]),
                            ALU.mult).then_inc(s_ready, 1)
            dve.wait_ge(sa_mm, 1)
            V.tensor_tensor(AM[0:32, :, 0:32], P[5][0:32, 0:128].rearrange("p (h s) -> p h s", h=GH),
                            cst("s_causal")[0:32].unsqueeze(1).to_broadcast([32, GH, 32]), ALU.mult).then_inc(sa_out, 1)
            def o_rstd(bs, n_squares, n_variance):
                dve.wait_ge(o_squares, n_squares)
                V.tensor_scalar(OSQ[:, bs], OSQ[:, bs], 1.0 / DV, EPS, ALU.mult, ALU.add).then_inc(variance, 1)
                dve.wait_ge(root, n_variance)
                link(V.reciprocal(ORS[:, bs], ORS[:, bs]))

            def gate_rows(bl, r):
                n = rows(bl)
                for h in range(GH):
                    c = slice(256 * h, 256 * h + 256)
                    ins = V.scalar_tensor_tensor(out=VG[0:n, bl, c], in0=VG[0:n, bl, c], scalar=ORS[0:n, bl, h:h + 1],
                                                 in1=r[0:n, c], op0=ALU.mult, op1=ALU.mult)
                ins.then_inc(g_rows, 1)

            dve.wait_ge(go_out, 8)
            o_rstd(slice(0, 4), 16, 2)
            dve.wait_ge(sk_out, 1)
            for h in range(GH):
                if h:
                    dve.wait_ge(su_mm, 2 * h)
                V.tensor_tensor(SKM[:], KHR[0:32, h, :].unsqueeze(1).to_broadcast([32, DB, 128]),
                                cst("row_batch")[0:32].unsqueeze(2).to_broadcast([32, DB, 128]), ALU.mult).then_inc(skm_ready, 1)
                for b in range(DB):
                    if b % 4 == 0:
                        dve.wait_ge(su_mm, 2 * h + b // 4 + 1)
                    st = (S0, S1)[h % 2][:, b, :]
                    V.scalar_tensor_tensor(out=st, in0=st, scalar=SEBL[:, h, b:b + 1],
                                           in1=P[4 + (b % 4) // 2][:, 256 * (b % 2):256 * (b % 2) + 256],
                                           op0=ALU.mult, op1=ALU.add).then_inc(su_out, 1)
                dve.wait_ge(r_in, 16 * (h + 1))
                gate_rows(h, RL)
            o_rstd(slice(4, 5), 20, 3)
            dve.wait_ge(so_out, GH)
            dve.wait_ge(rs_in, 16)
            gate_rows(4, RLS)
            dve.wait_ge(state_stored[0], 32)
            dve.wait_ge(state_stored[1], 32)
            dve.wait_ge(g_rows, NB)
            for bl in range(NB):
                lower_part(GT, G_BANKS, bl, gt_hi, gt_lo)
            V.memset(MT[:, :, :, NTOK:PADTOK].bitcast(F), 0.0)
            run_units(range(16, NU))
            dve.wait_ge(main_mm, unit_done(NU - 1))
            dve.wait_ge(squares, 3 * NB)
            link(V.tensor_tensor(SSQ[:], SSH[:, 0, :], SSH[:, 1, :], ALU.add))
            V.tensor_scalar(SSQ[:], SSQ[:], 1.0 / D, EPS, ALU.mult, ALU.add).then_inc(variance, 1)
            dve.wait_ge(root, 4)
            link(V.reciprocal(RST[:], RST[:]))
            dve.wait_ge(norm_in, 32)
            for bl in range(NB):
                n = rows(bl)
                if bl >= 2:
                    dve.wait_ge(h_turned, NB + bl - 1)
                    dve.wait_ge(h2_stored[bl % 2], 16 * (bl // 2))
                V.scalar_tensor_tensor(out=H2[0:n, bl % 2, :], in0=X2[0:n, bl, :], scalar=RST[0:n, bl:bl + 1],
                                       in1=NFFN[0:n, :], op0=ALU.mult, op1=ALU.mult).then_inc(h_rows, 1)
            L, lg = RR[0], RG[0]
            V.memset(ETF[:], 0.0)
            link(V.memset(L[:], 0.0))
            link(V.memset(lg[:], 0.0))
            dve.wait_ge(l_turned, 1)
            logits = P[6][:, 0:180].rearrange("p (b c) -> p b c", c=36)
            for r, bs in ((128, slice(0, 4)), (32, slice(4, 5))):
                nb = bs.stop - bs.start
                V.tensor_tensor(lg[0:r, bs, :], logits[0:r, bs, 0:NG], RB[0:r, 0:NG].unsqueeze(1).to_broadcast([r, nb, NG]), ALU.add)
                ins = V.tensor_tensor(L[0:r, bs, :], logits[0:r, bs, NG:36], RB[0:r, NG:36].unsqueeze(1).to_broadcast([r, nb, NE]), ALU.add)
            link(ins)

            def per_token(t, n):
                return t[:].unsqueeze(2).to_broadcast([128, NB, n])

            def per_expert(t):
                return t.unsqueeze(1).to_broadcast([128, NB, t.shape[-1]])

            def first_of_max(x, out, tmp, top, mark, rev, n):
                link(V.tensor_reduce(top[:], x[:], axis=AX.X, op=ALU.max))
                link(V.tensor_tensor(tmp[:], x[:], per_token(top, n), ALU.is_equal))
                link(V.tensor_tensor(tmp[:], tmp[:], per_expert(rev), ALU.mult))
                link(V.tensor_reduce(mark[:], tmp[:], axis=AX.X, op=ALU.max))
                link(V.tensor_tensor(out[:], tmp[:], per_token(mark, n), ALU.is_equal))

            first_of_max(lg, RG[1], RG[3], R1["gmax"], R1["grev"], cst("rev4"), NG)
            V.tensor_tensor(RG[2][:], lg[:], per_token(R1["gmax"], NG), ALU.subtract).then_inc(l_exp_in, 1)
            link(V.tensor_scalar(RG[3][:], RG[1][:], 1e30, -1e30, ALU.mult, ALU.add))
            ge = RR[1][:].rearrange("p b (g e) -> p b g e", g=NG)
            link(V.tensor_tensor(ge, L[:].rearrange("p b (g e) -> p b g e", g=NG), RG[3][:].unsqueeze(3).to_broadcast([128, NB, NG, EPG]), ALU.add))
            first_of_max(RR[1], RR[2], RR[5], R1["v1"], R1["m1"], cst("rev32"), NE)
            link(V.scalar_tensor_tensor(out=RR[1][:], in0=RR[2][:], scalar=-2e30, in1=RR[1][:], op0=ALU.mult, op1=ALU.add))
            first_of_max(RR[1], RR[3], RR[5], R1["v2"], R1["m2"], cst("rev32"), NE)
            V.tensor_tensor(R1["d"][:], R1["v2"][:], R1["v1"][:], ALU.subtract).then_inc(l_exp_in, 1)
            link(V.tensor_tensor(RR[4][:], RR[2][:], RR[3][:], ALU.add))
            V.tensor_tensor(RR[4][:], RR[4][:], cst("valid").unsqueeze(2).to_broadcast([128, NB, NE]), ALU.mult).then_inc(sel_ready, 1)
            dve.wait_ge(rank_mm, 1)
            rank, tot = RR[6], RR[7]
            link(V.tensor_copy(tot[:], P[5][:, 0:160].rearrange("p (b e) -> p b e", b=NB)))
            V.memset(RR[8][:, 0, :], 0.0)
            link(V.tensor_copy(RR[8][:, 1, :], tot[:, 0, :]))
            for b in range(2, NB):
                link(V.tensor_tensor(RR[8][:, b, :], RR[8][:, b - 1, :], tot[:, b - 1, :], ALU.add))
            V.tensor_tensor(RE1["count"][:], RR[8][:, 4, :], tot[:, 4, :], ALU.add)
            link(V.tensor_tensor(rank[:], P[4][:, 0:160].rearrange("p (b e) -> p b e", b=NB), RR[8][:], ALU.add))
            cmp = CMP[:, 0:NE * 8].rearrange("p (e s) -> p e s", s=8)
            link(V.tensor_tensor(cmp, RE1["count"][:].unsqueeze(2).to_broadcast([128, NE, 8]),
                                 cst("steps").unsqueeze(1).to_broadcast([128, NE, 8]), ALU.is_gt))
            link(V.tensor_reduce(RE1["tiles"][:], cmp, axis=AX.X, op=ALU.add))
            link(V.tensor_tensor_scan(out=RE1["cum"][:], data0=cst("ones")[:, 0:NE], data1=RE1["tiles"][:], initial=0.0,
                                      op0=ALU.mult, op1=ALU.add))
            link(V.tensor_tensor(RE1["start"][:], RE1["cum"][:], RE1["tiles"][:], ALU.subtract))
            for k, hot in enumerate((RR[2], RR[3])):
                for name, src in (("rank", rank[:]), ("place", per_expert(cst("place"))), ("over", per_expert(RE1["start"][:]))):
                    link(V.tensor_tensor(RR[9][:], hot[:], src, ALU.mult))
                    link(V.tensor_reduce(R2[name][:, NB * k:NB * k + NB], RR[9][:], axis=AX.X, op=ALU.add))
            cmp2 = CMP[:, 0:2 * NB * 8].rearrange("p (j s) -> p j s", s=8)
            link(V.tensor_tensor(cmp2, R2["rank"][:].unsqueeze(2).to_broadcast([128, 2 * NB, 8]),
                                 cst("steps").unsqueeze(1).to_broadcast([128, 2 * NB, 8]), ALU.is_ge))
            link(V.tensor_reduce(R2["q"][:], cmp2, axis=AX.X, op=ALU.add))
            link(V.scalar_tensor_tensor(out=R2["row"][:], in0=R2["q"][:], scalar=-float(CAP), in1=R2["rank"][:], op0=ALU.mult, op1=ALU.add))
            link(V.tensor_scalar(R2["isov"][:], R2["q"][:], 1.0, None, ALU.is_ge))
            link(V.scalar_tensor_tensor(out=R2["tile"][:], in0=R2["q"][:], scalar=-1.0, in1=R2["over"][:], op0=ALU.add, op1=ALU.add))
            link(V.tensor_scalar(R2["half"][:], R2["tile"][:], float(OVH), float(CAP * NPC - OVH), ALU.is_ge, ALU.mult))
            link(V.scalar_tensor_tensor(out=R2["a"][:], in0=R2["tile"][:], scalar=float(NFIX), in1=R2["half"][:], op0=ALU.add, op1=ALU.add))
            link(V.tensor_tensor(R2["a"][:], R2["a"][:], R2["place"][:], ALU.subtract))
            link(V.tensor_tensor(R2["a"][:], R2["a"][:], R2["isov"][:], ALU.mult))
            link(V.tensor_tensor(R2["a"][:], R2["a"][:], R2["place"][:], ALU.add))
            link(V.scalar_tensor_tensor(out=R2["pos"][:], in0=R2["row"][:], scalar=float(NPC), in1=R2["a"][:], op0=ALU.mult, op1=ALU.add))
            dve.wait_ge(tables_in, 16)
            V.tensor_copy(POSI[:], R2["pos"][:]).then_inc(pos_ready, 1)
            link(V.tensor_copy(ETF[:, 0:NFIX, :].rearrange("p t h -> p (t h)"), cst("expert")[0:1, :]))
            c3 = CMP[0:1, 0:MAXOV * NE].rearrange("p (t e) -> p t e", e=NE)
            link(V.tensor_tensor(c3, RE1["cum"][0:1, :].unsqueeze(1).to_broadcast([1, MAXOV, NE]),
                                 cst("ovtile")[0:1, :].unsqueeze(2).to_broadcast([1, MAXOV, NE]), ALU.is_le))
            link(V.tensor_reduce(EOV[:], c3, axis=AX.X, op=ALU.add))
            link(V.tensor_scalar(EOV[:], EOV[:], float(NE - 1), None, ALU.min))
            link(V.tensor_copy(ETF[:, NFIX:NFIX + OVH, :], EOV[:].rearrange("p (h t) -> p t h", h=2)))
            V.tensor_copy(ETI[:], ETF[:]).then_inc(iters_ready, 1)
            c4 = CMP[0:1, 0:OVH // 2]
            link(V.tensor_tensor(c4, RE1["cum"][0:1, NE - 1:NE].to_broadcast([1, OVH // 2]), cst("pairsteps")[0:1, :], ALU.is_gt))
            link(V.tensor_reduce(ITF[:], c4, axis=AX.X, op=ALU.add))
            link(V.tensor_scalar(ITF[:], ITF[:], float(NFIX // 2), None, ALU.add))
            V.tensor_copy(ITI[:], ITF[:]).then_inc(iters_ready, 1)
            dve.wait_ge(l_exp, 2)
            link(V.tensor_reduce(R1["gsum"][:], RG[2][:], axis=AX.X, op=ALU.add))
            link(V.reciprocal(R1["psel"][:], R1["gsum"][:]))
            link(V.tensor_scalar(R1["w1"][:], R1["e2"][:], 1.0, None, ALU.add))
            link(V.reciprocal(R1["w1"][:], R1["w1"][:]))
            link(V.tensor_tensor(R1["w1"][:], R1["w1"][:], R1["psel"][:], ALU.mult))
            link(V.tensor_tensor(R1["w2"][:], R1["w1"][:], R1["e2"][:], ALU.mult))
            for u in range(2):
                dve.wait_ge(scattered[u], 16)
            link(V.tensor_copy(IF1[:], IDXS[:]))
            link(V.tensor_scalar(IF2[:], IF1[:], float(NTOK), -float(NTOK), ALU.is_ge, ALU.mult))
            link(V.tensor_tensor(IF1[:], IF1[:], IF2[:], ALU.add))
            V.tensor_copy(IDXG[:], IF1[:]).then_inc(rows_ready, 1)
            turns = dve.value_load(ITI[0:1, 0:1], min_val=NFIX // 2, max_val=(NFIX + OVH) // 2)

            def xt_half(u):
                V.tensor_copy(XT[u][:, 4:8, :], P[1][:].rearrange("p (k n) -> p k n", k=4)).then_inc(xt_out_v, 1)

            dve.sem_inc(y_out_v, 1)
            dve.sem_inc(act_done, 1)
            dve.wait_ge(xg_turned, 2)
            xt_half(0)
            with dve.Fori(0, turns) as i:
                for u in range(2):
                    n = 2 * i + u
                    dve.wait_ge(silu_done, n + 1)
                    dve.wait_ge(act_turned, n + 1)
                    V.tensor_tensor(AC[u][:], SA[:], P[2 + u][:, FF:2 * FF], ALU.mult).then_inc(act_done, 1)
                    dve.wait_ge(act_turned, n + 2)
                    V.tensor_copy(ACTT[u][:], P[4 + u][:, 0:256].rearrange("p (j n) -> p j n", j=2)).then_inc(actt_out, 1)
                    dve.wait_ge(xg_turned, n + 3)
                    xt_half(1 - u)
                    dve.wait_ge(dn_done, n + 1)
                    dve.wait_ge(scattered[u], 16 * i + 16)
                    V.tensor_copy(YO[u][:, 512:1024], P[7][:]).then_inc(y_out_v, 1)
            dve.wait_ge(norm_in, 48)

            def add_experts(bl):
                n = rows(bl)
                y1, y2 = YI[2 * bl], YI[2 * bl + 1]
                dve.wait_ge(y_in[bl], 32)
                link(V.scalar_tensor_tensor(out=y1[0:n, :], in0=y1[0:n, :], scalar=R1["w1"][0:n, bl:bl + 1], in1=X2[0:n, bl, :],
                                            op0=ALU.mult, op1=ALU.add))
                V.scalar_tensor_tensor(out=y1[0:n, :], in0=y2[0:n, :], scalar=R1["w2"][0:n, bl:bl + 1], in1=y1[0:n, :],
                                       op0=ALU.mult, op1=ALU.add).then_inc(x3_ready, 1)

            def last_norm(bl):
                n = rows(bl)
                y1 = YI[2 * bl]
                dve.wait_ge(squares, 3 * NB + bl + 1)
                V.tensor_scalar(SSQ[:, bl:bl + 1], SSQ[:, bl:bl + 1], 1.0 / D, EPS, ALU.mult, ALU.add).then_inc(variance, 1)
                dve.wait_ge(root, 4 + bl + 1)
                link(V.reciprocal(RST[:, bl:bl + 1], RST[:, bl:bl + 1]))
                V.scalar_tensor_tensor(out=y1[0:n, :], in0=y1[0:n, :], scalar=RST[0:n, bl:bl + 1], in1=NFIN[0:n, :],
                                       op0=ALU.mult, op1=ALU.mult).then_inc(out_rows, 1)

            for bl in range(NB + 1):
                if bl < NB:
                    add_experts(bl)
                if bl:
                    last_norm(bl - 1)


INS = ["x_prompt", "x_sample", "cache_win_k", "cache_win_v", "state_gla", "norm_mix", "w_in", "w_gla_f2", "b_gla_f", "gla_norm",
       "attn_sinks", "w_proj_attn", "w_proj_gla", "w_out", "norm_ffn", "w_router_group", "b_router_group", "w_router_expert",
       "b_router_expert", "w_exp_gate", "w_exp_up", "w_exp_down", "norm_final"]
OUTS = [("y_prompt", (1, 512, D)), ("y_sample", (DB, DS, D)), ("prompt_win_k", (1, 1, WIN, KVH, HD)),
        ("prompt_win_v", (1, 1, WIN, KVH, HD)), ("prompt_gla_state", (1, 1, GH, DK, DV)),
        ("sample_win_k", (1, DB, WIN, KVH, HD)), ("sample_win_v", (1, DB, WIN, KVH, HD)),
        ("sample_gla_state", (1, DB, GH, DK, DV))]


def kernel(**inputs):
    import numpy as _np
    import concourse.bacc as _bacc
    from concourse import mybir as _mybir
    from concourse.bass_utils import run_bass_kernel_spmd as _run

    nc = _bacc.Bacc("TRN2", target_bir_lowering=False, num_devices=1)
    _, tables, rope, token_rows, empty = shape_constants()
    given = {n: _np.ascontiguousarray(inputs[n]) for n in INS}
    given.update(tables=tables, rope=rope, token_rows=token_rows, empty_slots=empty)
    a = {n: nc.dram_tensor(f"in_{n}", v.shape, _mybir.dt.from_np(v.dtype), kind="ExternalInput").ap() for n, v in given.items()}
    o = {n: nc.dram_tensor(f"out_{n}", s, _mybir.dt.float32, kind="ExternalOutput").ap() for n, s in OUTS}
    decoder_step(nc, a, o)
    r = _run(nc, [{f"in_{n}": v for n, v in given.items()}], core_ids=[0])
    return tuple(r.results[0][f"out_{n}"] for n, _ in OUTS)
```
